# Optimizing a Trainium2 kernel written in Bass

```python
import jax, jax.numpy as jnp
from jax import lax
import numpy as np

D_MODEL = 1024
BATCH = 1
SEQ = 4096
DEPTH = 1

CHUNK = 64
GLA_WIDTH = D_MODEL // 2
GLA_HEADS = 4
GLA_DV = GLA_WIDTH // GLA_HEADS
GLA_DK = GLA_DV // 2
GLA_KW = GLA_HEADS * GLA_DK
GLA_LOWRANK = 16
GLA_GATE_NORM = 16.0
HG_WIDTH = D_MODEL // 2
HG_EXPAND = 128
HG_HEADS = HG_WIDTH // HG_EXPAND
HG_DK = HG_EXPAND
HG_DV = HG_WIDTH // HG_HEADS
IN_WIDTHS = [GLA_KW, GLA_KW, GLA_WIDTH, GLA_WIDTH, GLA_LOWRANK,
             HG_WIDTH, HG_WIDTH, HG_WIDTH, HG_WIDTH, 2 * D_MODEL]
IN_TOTAL = int(sum(IN_WIDTHS))
IN_SPLITS = [int(s) for s in np.cumsum(IN_WIDTHS)[:-1]]
EPS = 1e-6
LB_FLOOR = 1e-30

kernel_name = "hybrid_gla_hgrn2_chunk_causal_adaln"

def rms_norm(x, w):
    xf = x.astype(jnp.float32)
    y = xf * lax.rsqrt(jnp.mean(xf * xf, axis=-1, keepdims=True) + EPS)
    return (y * w.astype(jnp.float32)).astype(x.dtype)

def chunk_gated_state(q, k, v, log_decay):
    B, S, H, dk = q.shape
    dv = v.shape[-1]
    N = S // CHUNK
    qc = q.reshape(B, N, CHUNK, H, dk)
    kc = k.reshape(B, N, CHUNK, H, dk).astype(jnp.float32)
    vc = v.reshape(B, N, CHUNK, H, dv).astype(jnp.float32)
    G = jnp.cumsum(log_decay.reshape(B, N, CHUNK, H, dk).astype(jnp.float32), axis=2)
    G_end = G[:, :, -1]
    k_dec = kc * jnp.exp(G_end[:, :, None] - G)
    dS = jnp.einsum('bnlhk,bnlhv->nbhkv', k_dec, vc)
    A = jnp.exp(jnp.transpose(G_end, (1, 0, 2, 3)))

    def step(S_prev, inp):
        a, d = inp
        S_new = a[..., None] * S_prev + d
        return S_new, S_new

    S0 = jnp.zeros((B, H, dk, dv), jnp.float32)
    _, S_all = lax.scan(step, S0, (A, dS))
    o = jnp.einsum('bnlhk,nbhkv->bnlhv', qc.astype(jnp.float32), S_all)
    return o.reshape(B, S, H, dv).astype(v.dtype)

def setup_inputs(seed: int = 0) -> dict:
    key = jax.random.key(seed)
    ks = jax.random.split(key, 16)
    D = D_MODEL
    nrm = jax.random.normal
    f32 = jnp.float32
    return {
        "x": nrm(ks[0], (BATCH, SEQ, D), f32),
        "c": nrm(ks[1], (BATCH, D), f32),
        "norm_w": 1.0 + 0.02 * nrm(ks[2], (DEPTH, D), f32),
        "ada_w": nrm(ks[3], (DEPTH, D, 3 * D), f32) * D ** -0.5,
        "ada_b": 0.02 * nrm(ks[4], (DEPTH, 3 * D), f32),
        "w_in": nrm(ks[5], (DEPTH, D, IN_TOTAL), f32) * D ** -0.5,
        "gla_wa2": nrm(ks[6], (DEPTH, GLA_LOWRANK, GLA_KW), f32) * GLA_LOWRANK ** -0.5,
        "gla_ba": 0.1 * nrm(ks[7], (DEPTH, GLA_KW), f32),
        "gla_norm_w": 1.0 + 0.02 * nrm(ks[8], (DEPTH, GLA_DV), f32),
        "hgrn_gamma": nrm(ks[9], (DEPTH, HG_WIDTH), f32),
        "hgrn_norm_w": 1.0 + 0.02 * nrm(ks[10], (DEPTH, HG_DV), f32),
        "merge_b": 0.02 * nrm(ks[11], (DEPTH, 2 * D), f32),
        "w_up_gla": nrm(ks[12], (DEPTH, GLA_WIDTH, D), f32) * GLA_WIDTH ** -0.5,
        "w_up_hgrn": nrm(ks[13], (DEPTH, HG_WIDTH, D), f32) * HG_WIDTH ** -0.5,
        "w_out": nrm(ks[14], (DEPTH, D, D), f32) * D ** -0.5,
        "final_norm_w": 1.0 + 0.02 * nrm(ks[15], (D,), f32),
    }

def reference(x, c, norm_w, ada_w, ada_b, w_in, gla_wa2, gla_ba, gla_norm_w, hgrn_gamma,
              hgrn_norm_w, merge_b, w_up_gla, w_up_hgrn, w_out, final_norm_w):
    B, S, _ = x.shape
    sm = jax.nn.softmax(hgrn_gamma.astype(jnp.float32), axis=0)
    lower_bounds = jnp.cumsum(sm, axis=0) - sm[0]
    c_act = jax.nn.silu(c)
    for l in range(DEPTH):
        mod = c_act @ ada_w[l] + ada_b[l]
        shift, scale, gate = jnp.split(mod, 3, axis=-1)
        h = rms_norm(x, norm_w[l]) * (1.0 + scale[:, None]) + shift[:, None]
        p = h @ w_in[l]
        gq, gk, gv, gz, glr, hq, hf, hi, hz, mg = jnp.split(p, IN_SPLITS, axis=-1)

        log_a = jax.nn.log_sigmoid((glr @ gla_wa2[l] + gla_ba[l]).astype(jnp.float32)) / GLA_GATE_NORM
        o_g = chunk_gated_state(
            (gq * GLA_DK ** -0.5).reshape(B, S, GLA_HEADS, GLA_DK),
            gk.reshape(B, S, GLA_HEADS, GLA_DK),
            gv.reshape(B, S, GLA_HEADS, GLA_DV),
            log_a.reshape(B, S, GLA_HEADS, GLA_DK))
        o_g = rms_norm(o_g, gla_norm_w[l]) * jax.nn.silu(gz.reshape(B, S, GLA_HEADS, GLA_DV))
        o_g = o_g.reshape(B, S, GLA_WIDTH)

        lb = jnp.clip(lower_bounds[l], 0.0, 1.0 - 1e-6)
        zf = hf.astype(jnp.float32)
        log_f = jnp.logaddexp(jnp.log(jnp.maximum(lb, LB_FLOOR)),
                              jnp.log1p(-lb) + jax.nn.log_sigmoid(zf))
        k_h = ((1.0 - lb) * jax.nn.sigmoid(-zf)).astype(x.dtype)
        o_h = chunk_gated_state(
            (jax.nn.silu(hq) * HG_DK ** -0.5).reshape(B, S, HG_HEADS, HG_DK),
            k_h.reshape(B, S, HG_HEADS, HG_DK),
            hi.reshape(B, S, HG_HEADS, HG_DV),
            log_f.reshape(B, S, HG_HEADS, HG_DK))
        o_h = rms_norm(o_h, hgrn_norm_w[l]) * jax.nn.silu(hz.reshape(B, S, HG_HEADS, HG_DV))
        o_h = o_h.reshape(B, S, HG_WIDTH)

        g_a, g_b = jnp.split(jax.nn.sigmoid(mg + merge_b[l]), 2, axis=-1)
        m = g_a * (o_g @ w_up_gla[l]) + g_b * (o_h @ w_up_hgrn[l])
        x = x + gate[:, None] * (m @ w_out[l])
    return rms_norm(x, final_norm_w)


_drawn_inputs = setup_inputs


def setup_inputs(seed=0):
    import zlib

    import numpy as np

    out = dict(_drawn_inputs(seed))
    spreads = {}
    factors = {'norm_w': 4.44,
     'gla_ba': 2.875,
     'gla_norm_w': 8.0,
     'hgrn_norm_w': 8.0,
     'merge_b': 8.0,
     'final_norm_w': 2.846}
    for name, (base, spread) in spreads.items():
        noise = np.random.default_rng([zlib.crc32(name.encode()), seed]).standard_normal(out[name].shape)
        drawn = base * np.exp(spread * noise) if base else spread * noise
        out[name] = __import__('jax').numpy.asarray(drawn.astype(out[name].dtype))
    for name, factor in factors.items():
        out[name] = (out[name] * factor).astype(out[name].dtype)
    return out
```

```python
import concourse.bass as bass
from concourse import mybir
from contextlib import ExitStack

P = 128
D = 1024
KT = D // P
T = 512
NT = T // P
CHUNK = 64
NC_BLK = T // CHUNK
LR = 16
GKW = 256
GW = GKW + LR
HEADS = 4
EPS = 1e-6
RAW, RING = 4, 3
SLOT_W = 4 * GW

F0, GK0, I0, GV0, GQ0, HQ0, GZ0, HZ0, MG0 = 0, 4, 6, 10, 14, 16, 20, 24, 28
MG_SLOT, UP_SLOT, _s = {}, {}, MG0
for _j in range(KT):
    for _g in range(2):
        MG_SLOT[_s] = (_j, _g)
        _s += 1
    if _j >= 1:
        UP_SLOT[_s] = _j - 1
        _s += 1
UP_SLOT[_s] = KT - 1
_s += 1
OUT0 = _s
SLOTS = OUT0 + 8
UP_AT = {j: s for s, j in UP_SLOT.items()}
MG_AT = {v: s for s, v in MG_SLOT.items()}
STEP_AT = [GZ0 - 1 + i for i in range(8)]
XT_AT = [53, 54, 56, 57]
assert SLOTS == 60 and SLOTS % RAW == 0 and SLOTS % RING == 0

ACT_LINKS, DVE_LINKS = 14, 25


def slot_width(s):
    return SLOT_W if GK0 <= s < I0 else 1024


class Signal:

    def __init__(self, sem, per, head=0):
        self.sem, self.per, self.head = sem, per, head

    def at(self, b, n):
        return b * self.per + (self.head + n)


def build(nc, x, mod_in, cols, rows, w_stream, ada, out):
    fp32, f32r = mybir.dt.float32, mybir.dt.float32r
    ALU, ACT, AX = mybir.AluOpType, mybir.ActivationFunctionType, mybir.AxisListType
    NB = x.shape[0] // T

    ctx = ExitStack()
    with ctx:
        base = nc.sbuf_base
        top = [(base + 31) // 32 * 32]

        def sb(name, shape, dt, at=None):
            size = 4
            for n in shape[1:]:
                size *= n
            if at is None:
                at = top[0]
                top[0] = (at + size + 31) // 32 * 32
            return nc.alloc_sbuf_tensor_at(name, shape, dt, offset=at)

        def here():
            return top[0]

        def sem(name):
            return ctx.enter_context(nc.semaphore(name))

        def signal(name, per, head=0):
            return Signal(sem(name), per, head)

        h_hi = sb("h_hi", [P, KT, T], f32r)
        h_lo = sb("h_lo", [P, KT, T], f32r)
        w_raw = sb("w_raw", [P, RAW, SLOT_W], fp32)
        w_hi = sb("w_hi", [P, RING, SLOT_W], f32r)
        w_lo = sb("w_lo", [P, RING, SLOT_W], f32r)
        o_at = here()
        o_hi = sb("o_hi", [P, 2 * HEADS, T], f32r)
        o_lo = sb("o_lo", [P, 2 * HEADS, T], f32r)
        z_f = sb("z_f", [P, NT, 512], fp32, at=o_at)
        t1 = sb("t1", [P, NT, 512], fp32, at=o_at + 8192)
        pk = sb("pk", [P, NT, 512], fp32, at=o_at + 16384)
        y_g = sb("y_g", [P, NT, GKW], fp32, at=o_at + 24576)
        t3 = sb("t3", [P, NT, GKW], fp32, at=o_at + 28672)
        ada_w = sb("ada_w", [P, 2, KT, 512], fp32, at=o_at)
        m_at = here()
        m_hi = sb("m_hi", [P, KT, T], f32r)
        m_lo = sb("m_lo", [P, KT, T], f32r)
        kdec_h = sb("kdec_h", [P, NT, 512], fp32, at=m_at)
        v_h = sb("v_h", [P, NT, 512], fp32, at=m_at + 8192)
        v_g = sb("v_g", [P, NT, 512], fp32, at=m_at + 16384)
        gklr = sb("gklr", [P, NT, GW], fp32, at=m_at + 24576)
        mod_bc = sb("mod_bc", [P, 3 * D], fp32, at=m_at)
        ada_b = sb("ada_b", [P, 3 * D], fp32, at=m_at + 12288)
        q_at = here()
        q_h = sb("q_h", [P, HEADS, T], fp32)
        xn = sb("xn", [P, 2, D], fp32, at=q_at)
        q_g = sb("q_g", [P, 2, T], fp32)
        oraw_at = here()
        o_tm = sb("o_tm", [P, NT, 2 * 512], fp32)
        xy = sb("xy", [P, NT, D], fp32, at=oraw_at)
        S_h = sb("S_h", [P, 2, HEADS, P], fp32)
        S_g = sb("S_g", [P, 2, 2, 2, P], fp32)
        a_cols = sb("a_cols", [P, 6, NC_BLK], fp32)
        gates_at = here()
        gates = sb("gates", [P, 2, 2, T], fp32)
        lrT = sb("lrT", [LR, T], fp32, at=gates_at)
        h_tmp_at = here()
        h_tmp = sb("h_tmp", [P, KT, P], fp32)
        a_rows = sb("a_rows", [NC_BLK, 768], fp32, at=h_tmp_at)
        row_bc = sb("row_bc", [P, 4, 512], fp32)
        c1, c2, c3 = row_bc[:, 0, :], row_bc[:, 1, :], row_bc[:, 2, :]
        ba_bc = row_bc[:, 3, 0:GKW]
        gate_bc = sb("gate_bc", [P, D], fp32)
        fnw_bc = sb("fnw_bc", [P, D], fp32)
        ident = sb("ident", [P, P], fp32)
        tri = sb("tri", [P, 2, P], fp32)
        ind = sb("ind", [P, 2, NT, NC_BLK], fp32)
        wa2 = sb("wa2", [LR, GKW], fp32)
        n_cols = cols.shape[1]
        col = sb("col", [P, n_cols], fp32)
        cT, norm_w, merge_b, nw = col[:, 0:8], col[:, 8:16], col[:, 16:32], col[:, 32:34]
        a_col = sb("a_col", [P, KT], fp32)
        s_col = sb("s_col", [P, 2 * KT], fp32)
        small = sb("small", [P, 8], fp32)
        c_act = sb("c_act", [P, KT], fp32)
        mhalf = sb("mhalf", [P, 16], fp32)
        eps_t = sb("eps_t", [P, 16], fp32)
        ssq = sb("ssq", [P, 2, 16], fp32)
        rstd = sb("rstd", [P, 2, 16], fp32)
        x_ss = sb("x_ss", [P, NT], fp32)
        x_rs = sb("x_rs", [P, NT], fp32)
        y_ss = sb("y_ss", [P, NT], fp32)
        y_rs = sb("y_rs", [P, NT], fp32)
        assert top[0] <= nc.sbuf_usable_end, (top[0], nc.sbuf_usable_end)

        def bank(name):
            return ctx.enter_context(nc.psum_tensor(name, [P, 512], fp32))

        A = [bank(f"A{i}") for i in range(4)]
        F = [bank(f"F{i}") for i in range(2)]
        R = [bank(f"R{i}") for i in range(2)]

        raw_in = [signal(f"raw_in{r}", SLOTS // RAW * 16) for r in range(RAW)]
        w_hi_done = signal("w_hi_done", SLOTS)
        w_split = signal("w_split", SLOTS)
        slot_done = signal("slot_done", SLOTS)
        a_done = signal("a_done", 24)
        f_copied = signal("f_copied", 4)
        gk_copied = signal("gk_copied", 4)
        i_copied = signal("i_copied", 4)
        gv_copied = signal("gv_copied", 4)
        z_sig = signal("z_sig", 8)
        z_used = signal("z_used", 8)
        gq_used = signal("gq_used", 2)
        hq_sig = signal("hq_sig", 4)
        hq_used = signal("hq_used", 4)
        mg_used = signal("mg_used", 16, 16)
        up_used = signal("up_used", 8)
        m_hi_done = signal("m_hi_done", 8)
        m_split = signal("m_split", 8)
        out_used = signal("out_used", 8, 8)
        lrT_done, lrT_copied = signal("lrT_done", 1), signal("lrT_copied", 1)
        y_done, y_added = signal("y_done", 1), signal("y_added", 1)
        g_act = signal("g_act", 1)
        log_a_ready = signal("log_a_ready", 1)
        f_act = signal("f_act", 2)
        f_dve = signal("f_dve", 1)
        log_f_ready = signal("log_f_ready", 1)
        grev_h_done, grev_h_used = signal("grev_h_done", 4), signal("grev_h_used", 4)
        kexp_h = signal("kexp_h", 1)
        kdec_h_ready = signal("kdec_h_ready", 1)
        grev_g_done, kexp_g = signal("grev_g_done", 1), signal("kexp_g", 2)
        kdec_g_ready = signal("kdec_g_ready", 1)
        gend_done, a_rows_ready = signal("gend_done", 1), signal("a_rows_ready", 2)
        aT_done, a_ready = signal("aT_done", 1), signal("a_ready", 1)
        dS_done, S_ready = signal("dS_done", 8), signal("S_ready", 8)
        o_done, o_copied = signal("o_done", 8), signal("o_copied", 8)
        o_sq, ssq_done = signal("o_sq", 8), signal("ssq_done", 8)
        rstd_ready = signal("rstd_ready", 2)
        og_ready = signal("og_ready", 2)
        oT_done = signal("oT_done", 8)
        o_hi_done, o_split = signal("o_hi_done", 8), signal("o_split", 8)
        xn_in = [signal(f"xn_in{r}", 32) for r in range(2)]
        x_sq = signal("x_sq", 4)
        x_rstd = signal("x_rstd", 4)
        x_normed = signal("x_normed", 4)
        xT_done = signal("xT_done", 4)
        h_affine = signal("h_affine", 4)
        h_hi_done, h_split = signal("h_hi_done", 4), signal("h_split", 4)
        xy_in = signal("xy_in", 16)
        y_sum = signal("y_sum", 4)
        y_sq, y_rstd, y_ready = signal("y_sq", 4), signal("y_rstd", 4), signal("y_ready", 4)
        out_stored = signal("out_stored", 64, 64)
        act_link, dve_link = sem("act_link"), sem("dve_link")
        const_in, pool_link, consts = sem("const_in"), sem("pool_link"), sem("consts")
        ada_in = [sem("ada_in0"), sem("ada_in1")]
        ada_pe, ada_dve, c_ready, modT, mod_ready = (sem("ada_pe"), sem("ada_dve"), sem("c_ready"),
                                                     sem("modT"), sem("mod_ready"))
        act_pre, dve_pre, pool_pow = sem("act_pre"), sem("dve_pre"), sem("pool_pow")

        def wait_tile(eng, b, group, t, s):
            if t < 3:
                eng.wait_ge(a_done.sem, a_done.at(b, 3 * group + t + 1))
            else:
                eng.wait_ge(slot_done.sem, slot_done.at(b, s + 1))

        block = ctx.enter_context(nc.Block())

        @block.sync
        def _(sp):
            def load_w(s):
                r = s % RAW
                sp.dma_start(w_raw[:, r, 0:slot_width(s)],
                             w_stream[s, :, 0:slot_width(s)]).then_inc(raw_in[r].sem, 16)

            def load_x(nb, t):
                sp.dma_start(xn[:, t % 2, :],
                             x[bass.ds(nb * T + t * P, P), :]).then_inc(xn_in[t % 2].sem, 16)

            sp.sem_inc(out_stored.sem, 64)
            sp.dma_start(col[:, :], cols[:, :]).then_inc(const_in, 16)
            sp.dma_start(row_bc[:, 0, :], rows[0:1, 0:512].partition_broadcast(P)
                         .rearrange("p a n -> p (a n)")).then_inc(const_in, 16)
            sp.dma_start(ba_bc, rows[0:1, 512:512 + GKW].partition_broadcast(P)
                         .rearrange("p a n -> p (a n)")).then_inc(const_in, 16)
            sp.dma_start(fnw_bc[:, :], rows[0:1, 768:768 + D].partition_broadcast(P)
                         .rearrange("p a n -> p (a n)")).then_inc(const_in, 16)
            sp.dma_start(ada_b[:, :], rows[0:1, 1792:1792 + 3 * D].partition_broadcast(P)
                         .rearrange("p a n -> p (a n)")).then_inc(const_in, 16)
            sp.dma_start(wa2[:, :], mod_in[:, :]).then_inc(const_in, 16)
            load_x(0, 0)
            load_x(0, 1)
            for n in range(6):
                if n >= 2:
                    sp.wait_ge(ada_pe, n - 1)
                sp.dma_start(ada_w[:, n % 2, :, :],
                             ada[n, :, :].rearrange("p (k n) -> p k n", k=KT)).then_inc(ada_in[n % 2], 16)
            for s in range(RAW):
                load_w(s)
            for t in (2, 3):
                sp.wait_ge(xT_done.sem, xT_done.at(0, t - 1))
                load_x(0, t)

            def body(b, last):
                for s in range(SLOTS):
                    if not (last and s + RAW >= SLOTS):
                        sp.wait_ge(w_split.sem, w_split.at(b, s + 1))
                        load_w((s + RAW) % SLOTS)
                    if s == 38:
                        sp.wait_ge(slot_done.sem, slot_done.at(b, UP_AT[0] + 1))
                        sp.dma_start(xy[:, :, :], x[bass.ds(b * T, T), :]
                                     .rearrange("(t p) d -> p t d", p=P)).then_inc(xy_in.sem, 16)
                    if s in (39, 40) and not last:
                        load_x(b + 1, s - 39)
                    if s in (57, 58) and not last:
                        sp.wait_ge(xT_done.sem, xT_done.at(b + 1, s - 56))
                        load_x(b + 1, s - 55)
                for t in range(NT):
                    sp.wait_ge(y_ready.sem, y_ready.at(b, t + 1))
                    sp.dma_start(out[bass.ds(b * T + t * P, P), :], xy[:, t, :]).then_inc(out_stored.sem, 16)

            with sp.Fori(0, NB - 1) as b:
                body(b, False)
            body(NB - 1, True)
            sp.wait_ge(out_stored.sem, out_stored.at(NB, 0))

        @block.gpsimd
        def _(pool):
            links = [0]

            def link(ins):
                links[0] += 1
                ins.then_inc(pool_link, 1)
                pool.wait_ge(pool_link, links[0])

            link(nc.gpsimd.memset(ident[:, :], 0.0))
            link(nc.gpsimd.affine_select(out=ident[:, :], in_=ident[:, :], compare_op=ALU.not_equal, fill=1.0,
                                         base=0, pattern=[[-1, P]], channel_multiplier=1))
            for v, val in ((0, 1.0), (1, 1.0 / 16.0)):
                link(nc.gpsimd.memset(tri[:, v, :], val))
                link(nc.gpsimd.affine_select(out=tri[:, v, :], in_=tri[:, v, :], compare_op=ALU.is_gt, fill=0.0,
                                             base=0, pattern=[[-1, P]], channel_multiplier=1))
                link(nc.gpsimd.memset(tri[CHUNK:P, v, 0:CHUNK], 0.0))
                link(nc.gpsimd.memset(ind[:, v, :, :], 0.0))
                for t in range(NT):
                    for c in range(2):
                        link(nc.gpsimd.memset(ind[c * CHUNK:(c + 1) * CHUNK, v, t, 2 * t + c:2 * t + c + 1], val))
            link(nc.gpsimd.memset(mhalf[:, :], -0.5))
            link(nc.gpsimd.memset(eps_t[:, :], EPS))
            link(nc.gpsimd.memset(S_h[:, :, :, :], 0.0))
            nc.gpsimd.memset(S_g[:, :, :, :, :], 0.0).then_inc(consts, 1)

            pw = [0]

            def inverse_root(dst, src, ready):
                k = dst.shape[1]
                nc.gpsimd.tensor_tensor(dst, src, eps_t[:, 0:k], ALU.add).then_inc(pool_pow, 1)
                pw[0] += 1
                pool.wait_ge(pool_pow, pow_base(pw[0]))
                nc.gpsimd.tensor_tensor(dst, dst, mhalf[:, 0:k], ALU.pow).then_inc(ready.sem, 1)

            pow_base = lambda n: n

            def x_tile(nb, t):
                pool.wait_ge(x_sq.sem, x_sq.at(nb, t + 1))
                inverse_root(x_rs[:, t:t + 1], x_ss[:, t:t + 1], x_rstd)

            for t in range(NT):
                x_tile(0, t)

            head = pw[0]
            PER = 2 + 2 * NT

            def body(b, last):
                nonlocal pow_base
                pw[0] = 0
                pow_base = lambda n: b * PER + (head + n)
                for fam in range(2):
                    pool.wait_ge(ssq_done.sem, ssq_done.at(b, 4 * fam + 4))
                    inverse_root(rstd[:, fam, :], ssq[:, fam, :], rstd_ready)
                if not last:
                    for t in range(NT):
                        x_tile(b + 1, t)
                for t in range(NT):
                    pool.wait_ge(y_sq.sem, y_sq.at(b, t + 1))
                    inverse_root(y_rs[:, t:t + 1], y_ss[:, t:t + 1], y_rstd)

            with pool.Fori(0, NB - 1) as b:
                body(b, False)
            body(NB - 1, True)

        @block.scalar
        def _(act):
            AF = nc.scalar.activation
            link_at = [None, 0, 0]

            def link(ins):
                link_at[1] += 1
                ins.then_inc(act_link, 1)
                act.wait_ge(act_link, link_at[0] * ACT_LINKS + (link_at[2] + link_at[1])
                            if link_at[0] is not None else link_at[1])

            def split_hi(b, s):
                act.wait_ge(raw_in[s % RAW].sem, raw_in[s % RAW].at(b, (s // RAW + 1) * 16))
                n = slot_width(s)
                AF(w_hi[:, s % RING, 0:n], w_raw[:, s % RAW, 0:n], ACT.Copy).then_inc(w_hi_done.sem, 1)

            def x_square(nb, t):
                act.wait_ge(xn_in[t % 2].sem, xn_in[t % 2].at(nb, (t // 2 + 1) * 16))
                link(AF(gates[:, 0, :, :].rearrange("p a n -> p (a n)"), xn[:, t % 2, :], ACT.Square, scale=D ** -0.5,
                        accum_out=x_ss[:, t:t + 1]))
                nc.scalar.activation(small[:, 0:1], x_ss[:, t:t + 1], ACT.Copy).then_inc(x_sq.sem, 1)

            def h_high(nb, t):
                act.wait_ge(h_affine.sem, h_affine.at(nb, t + 1))
                AF(h_hi[:, :, t * P:(t + 1) * P], h_tmp[:, :, :], ACT.Copy).then_inc(h_hi_done.sem, 1)

            act.wait_ge(const_in, 96)
            link(AF(c_act[:, :], cT, ACT.Sigmoid))
            nc.scalar.activation(small[:, 0:1], c_act[:, 0:1], ACT.Copy).then_inc(act_pre, 1)
            for t in (0, 1):
                x_square(0, t)
            act.wait_ge(dve_pre, 1)
            link(AF(c1, c1, ACT.Ln))
            AF(c2, c3, ACT.Ln).then_inc(act_pre, 1)
            for s in range(RING):
                split_hi(0, s)
            for t in range(NT):
                if t >= 2:
                    x_square(0, t)
                h_high(0, t)
            link_at[2] = link_at[1]

            def softplus_abs(buf, signals):
                link(AF(buf, buf, ACT.Abs))
                link(AF(buf, buf, ACT.Exp, scale=-1.0))
                AF(buf, buf, ACT.Ln, bias=1.0).then_inc(signals.sem, 1)

            flat = lambda t: t[:, :, :].rearrange("p t n -> p (t n)")

            def body(b, last):
                link_at[0], link_at[1] = b, 0
                for s in range(SLOTS):
                    if s == F0 + 3:
                        for t in range(NT):
                            wait_tile(act, b, 0, t, s)
                            AF(z_f[:, t, :], A[t][:, :], ACT.Copy).then_inc(f_copied.sem, 1)
                    if s == GK0 + 1:
                        for t in range(NT):
                            wait_tile(act, b, 1, t, s)
                            AF(gklr[:, t, :], A[t][:, 0:GW], ACT.Copy).then_inc(gk_copied.sem, 1)
                    if s == I0 + 3:
                        for t in range(NT):
                            wait_tile(act, b, 2, t, s)
                            AF(v_h[:, t, :], A[t][:, :], ACT.Copy).then_inc(i_copied.sem, 1)
                    if s == GV0 + 3:
                        for t in range(NT):
                            wait_tile(act, b, 3, t, s)
                            AF(v_g[:, t, :], A[t][:, :], ACT.Copy).then_inc(gv_copied.sem, 1)
                    for fam, at in ((0, GZ0 + 3), (1, HZ0 + 3)):
                        if s == at:
                            if fam:
                                act.wait_ge(og_ready.sem, og_ready.at(b, 1))
                            for t in range(NT):
                                wait_tile(act, b, 4 + fam, t, s)
                                AF(v_g[:, t, :], A[t][:, :], ACT.Sigmoid).then_inc(z_sig.sem, 1)
                    act.wait_ge(slot_done.sem, slot_done.at(b, s + 1))
                    if GQ0 <= s < HQ0:
                        n = s - GQ0
                        AF(q_g[:, n, :], F[n % 2][:, :], ACT.Copy, scale=0.125).then_inc(gq_used.sem, 1)
                    if HQ0 <= s < GZ0:
                        n = s - HQ0
                        if n >= 2:
                            act.wait_ge(hq_used.sem, hq_used.at(b, n - 1))
                        AF(gates[:, 0, n % 2, :], F[n % 2][:, :], ACT.Sigmoid).then_inc(hq_sig.sem, 1)
                    if s in MG_SLOT:
                        j, g = MG_SLOT[s]
                        if j >= 2 and g == 0:
                            act.wait_ge(m_split.sem, m_split.at(b, j - 1))
                        AF(gates[:, j % 2, g, :], F[g][:, :], ACT.Sigmoid,
                           bias=merge_b[:, g * KT + j:g * KT + j + 1]).then_inc(mg_used.sem, 1)
                    if not (last and s + RING >= SLOTS):
                        split_hi(b if s + RING < SLOTS else b + 1, (s + RING) % SLOTS)
                    if s in UP_SLOT:
                        j = UP_SLOT[s]
                        act.wait_ge(up_used.sem, up_used.at(b, j + 1))
                        AF(m_hi[:, j, :], gates[:, j % 2, 0, :], ACT.Copy).then_inc(m_hi_done.sem, 1)
                    if s == 4:
                        act.wait_ge(f_copied.sem, f_copied.at(b, 4))
                        link(AF(flat(t1), flat(z_f), ACT.Abs))
                    if s == 5:
                        link(AF(flat(t1), flat(t1), ACT.Exp, scale=-1.0))
                        AF(flat(t1), flat(t1), ACT.Ln, bias=1.0).then_inc(f_act.sem, 1)
                    if s == 9:
                        act.wait_ge(f_dve.sem, f_dve.at(b, 1))
                        link(AF(flat(t1), flat(t1), ACT.Abs))
                    if s == 10:
                        link(AF(flat(t1), flat(t1), ACT.Exp, scale=-1.0))
                        AF(flat(t1), flat(t1), ACT.Ln, bias=1.0).then_inc(f_act.sem, 1)
                    if s == 7:
                        act.wait_ge(lrT_done.sem, lrT_done.at(b, 1))
                        AF(lrT[:, :], R[0][0:LR, :], ACT.Copy).then_inc(lrT_copied.sem, 1)
                    if s == 11:
                        act.wait_ge(y_added.sem, y_added.at(b, 1))
                        link(AF(flat(t3), flat(y_g), ACT.Abs))
                        link(AF(flat(t3), flat(t3), ACT.Exp, scale=-1.0))
                        AF(flat(t3), flat(t3), ACT.Ln, bias=1.0).then_inc(g_act.sem, 1)
                    if s == 14:
                        act.wait_ge(grev_g_done.sem, grev_g_done.at(b, 1))
                        for n in range(2):
                            AF(t3[:, 2 * n:2 * n + 2, :].rearrange("p t n -> p (t n)"), R[n][:, :],
                               ACT.Exp).then_inc(kexp_g.sem, 1)
                    if s == 15:
                        act.wait_ge(grev_h_used.sem, grev_h_used.at(b, 4))
                        AF(flat(pk), flat(pk), ACT.Exp).then_inc(kexp_h.sem, 1)
                        act.wait_ge(gend_done.sem, gend_done.at(b, 1))
                        AF(a_rows[:, 0:512], R[0][0:NC_BLK, :], ACT.Exp).then_inc(a_rows_ready.sem, 1)
                        AF(a_rows[:, 512:768], R[1][0:NC_BLK, 0:GKW], ACT.Exp).then_inc(a_rows_ready.sem, 1)
                    for i in range(8):
                        if s == STEP_AT[i] + 1:
                            fam, t = divmod(i, 4)
                            if i == 0:
                                act.wait_ge(out_stored.sem, out_stored.at(b, 0))
                            act.wait_ge(o_done.sem, o_done.at(b, i + 1))
                            AF(o_tm[:, t, fam * 512:(fam + 1) * 512], (F[0] if i < 7 else R[0])[:, :],
                               ACT.Copy).then_inc(o_copied.sem, 1)
                            act.wait_ge(o_copied.sem, o_copied.at(b, i + 1))
                            if i:
                                act.wait_ge(ssq_done.sem, ssq_done.at(b, i))
                            AF(h_tmp[:, 0:4, :].rearrange("p a n -> p (a n)"),
                               o_tm[:, t, fam * 512:(fam + 1) * 512], ACT.Square,
                               scale=P ** -0.5).then_inc(o_sq.sem, 1)
                    for i in range(8):
                        if s == (29, 29, 29, 29, 30, 30, 31, 31)[i]:
                            fam, t = divmod(i, 4)
                            act.wait_ge(oT_done.sem, oT_done.at(b, i + 1))
                            src = A[t] if fam == 0 else R[t % 2]
                            AF(o_hi[:, 4 * fam:4 * fam + 4, t * P:(t + 1) * P],
                               src[:, :].rearrange("p (a n) -> p a n", a=4), ACT.Copy,
                               scale=nw[:, fam:fam + 1]).then_inc(o_hi_done.sem, 1)
                    if not last:
                        if s == 52:
                            act.wait_ge(m_split.sem, m_split.at(b, 8))
                            x_square(b + 1, 0)
                            act.wait_ge(x_sq.sem, x_sq.at(b + 1, 1))
                            x_square(b + 1, 1)
                        if s == 54:
                            h_high(b + 1, 0)
                        if s == 55:
                            act.wait_ge(x_sq.sem, x_sq.at(b + 1, 2))
                            x_square(b + 1, 2)
                            h_high(b + 1, 1)
                        if s == 56:
                            act.wait_ge(x_sq.sem, x_sq.at(b + 1, 3))
                            x_square(b + 1, 3)
                        if s == 57:
                            h_high(b + 1, 2)
                        if s == 58:
                            h_high(b + 1, 3)
                    if s == 59:
                        for t in range(NT):
                            act.wait_ge(y_sum.sem, y_sum.at(b, t + 1))
                            link(AF(gates[:, 1, :, :].rearrange("p a n -> p (a n)"), xy[:, t, :], ACT.Square, scale=D ** -0.5,
                                    accum_out=y_ss[:, t:t + 1]))
                            nc.scalar.activation(small[:, 1:2], y_ss[:, t:t + 1], ACT.Copy).then_inc(y_sq.sem, 1)
                assert last or link_at[1] == ACT_LINKS, f"ACT_LINKS {link_at[1]}"

            with act.Fori(0, NB - 1) as b:
                body(b, False)
            body(NB - 1, True)

        @block.vector
        def _(dve):
            V = nc.vector
            link_at = [None, 0, 0]

            def link(ins):
                link_at[1] += 1
                ins.then_inc(dve_link, 1)
                dve.wait_ge(dve_link, link_at[0] * DVE_LINKS + (link_at[2] + link_at[1])
                            if link_at[0] is not None else link_at[1])

            def split_lo(b, s):
                dve.wait_ge(w_hi_done.sem, w_hi_done.at(b, s + 1))
                n = slot_width(s)
                V.tensor_tensor(w_lo[:, s % RING, 0:n], w_raw[:, s % RAW, 0:n],
                                w_hi[:, s % RING, 0:n].bitcast(fp32), ALU.subtract).then_inc(w_split.sem, 1)

            def x_norm(nb, t):
                dve.wait_ge(x_rstd.sem, x_rstd.at(nb, t + 1))
                V.tensor_scalar(xn[:, t % 2, :], xn[:, t % 2, :], x_rs[:, t:t + 1], None,
                                ALU.mult).then_inc(x_normed.sem, 1)

            def h_mod(nb, t):
                dve.wait_ge(xT_done.sem, xT_done.at(nb, t + 1))
                for k in range(KT):
                    last = V.tensor_scalar(h_tmp[:, k, :], R[k // 4][:, (k % 4) * P:(k % 4 + 1) * P],
                                           a_col[:, k:k + 1], s_col[:, k:k + 1], ALU.mult, ALU.add)
                last.then_inc(h_affine.sem, 1)

            def h_low(nb, t):
                dve.wait_ge(h_hi_done.sem, h_hi_done.at(nb, t + 1))
                V.tensor_tensor(h_lo[:, :, t * P:(t + 1) * P], h_tmp[:, :, :],
                                h_hi[:, :, t * P:(t + 1) * P].bitcast(fp32), ALU.subtract).then_inc(h_split.sem, 1)
                dve.wait_ge(h_split.sem, h_split.at(nb, t + 1))

            link(V.memset(small[:, 4:5], 0.0))
            dve.wait_ge(const_in, 96)
            dve.wait_ge(act_pre, 1)
            V.tensor_tensor(c_act[:, :], c_act[:, :], cT, ALU.mult).then_inc(c_ready, 1)
            link(V.tensor_tensor(c2, c1, c1, ALU.subtract))
            link(V.tensor_scalar(c2, c2, 1.0, None, ALU.add))
            link(V.reciprocal(c3, c2))
            link(V.tensor_tensor(c2, c2, c3, ALU.mult))
            link(V.tensor_tensor(c1, c2, c2, ALU.subtract))
            link(V.tensor_scalar(c1, c1, 0.0, 1.0 - 1e-6, ALU.max, ALU.min))
            link(V.tensor_scalar(c3, c1, -1.0, 1.0, ALU.mult, ALU.add))
            V.tensor_scalar(c1, c1, 1e-30, float(2 ** 50), ALU.max, ALU.mult).then_inc(dve_pre, 1)
            for t in (0, 1):
                x_norm(0, t)
            dve.wait_ge(act_pre, 2)
            link(V.tensor_scalar(c1, c1, -34.657359027997264, None, ALU.add))
            for n in range(6):
                dve.wait_ge(ada_pe, n + 1)
                V.tensor_tensor(mod_bc[:, n * 512:(n + 1) * 512], A[n % 4][:, :],
                                ada_b[:, n * 512:(n + 1) * 512], ALU.add).then_inc(ada_dve, 1)
            dve.wait_ge(ada_dve, 6)
            V.tensor_copy(gate_bc[:, :], mod_bc[:, 2 * D:3 * D])
            dve.wait_ge(modT, 1)
            for g in range(4):
                src = (A[0], A[1], F[0], F[1])[g]
                link(V.tensor_copy(s_col[:, 4 * g:4 * g + 4], src[:, 0:512:P]))
            link(V.tensor_scalar(a_col[:, :], s_col[:, KT:2 * KT], 1.0, None, ALU.add))
            V.tensor_tensor(a_col[:, :], a_col[:, :], norm_w, ALU.mult).then_inc(mod_ready, 1)
            dve.wait_ge(mod_ready, 1)
            for s in range(RING):
                split_lo(0, s)
            for t in range(NT):
                if t >= 2:
                    x_norm(0, t)
                h_mod(0, t)
                h_low(0, t)
            link(V.memset(small[:, 5:6], 0.0))
            V.memset(small[:, 6:7], 0.0).then_inc(mg_used.sem, 16)
            V.memset(small[:, 7:8], 0.0).then_inc(out_used.sem, 8)
            link_at[2] = link_at[1]

            def over_tiles(row, n):
                return row.unsqueeze(1).broadcast_to([P, NT, n])

            def body(b, last):
                link_at[0], link_at[1] = b, 0
                for s in range(SLOTS):
                    if s in (GZ0 + 3, HZ0 + 3):
                        fam = (s - GZ0) // 4
                        for t in range(NT):
                            dve.wait_ge(z_sig.sem, z_sig.at(b, 4 * fam + t + 1))
                            V.tensor_tensor(v_g[:, t, :], A[t][:, :], v_g[:, t, :],
                                            ALU.mult).then_inc(z_used.sem, 1)
                    if s in (OUT0 + 3, OUT0 + 7):
                        n = (s - OUT0) // 4
                        if n == 0:
                            dve.wait_ge(xy_in.sem, xy_in.at(b, 16))
                        for t in range(NT):
                            wait_tile(dve, b, 6 + n, t, s)
                            cols_ = slice(n * 512, (n + 1) * 512)
                            y_tmp = q_g[:, t % 2, :]
                            V.tensor_tensor(y_tmp, A[t][:, :], gate_bc[:, cols_], ALU.mult).then_inc(out_used.sem, 1)
                            dve.wait_ge(out_used.sem, out_used.at(b, 4 * n + t + 1))
                            ins = V.tensor_tensor(xy[:, t, cols_], xy[:, t, cols_], y_tmp, ALU.add)
                            if n:
                                ins.then_inc(y_sum.sem, 1)
                            else:
                                link(ins)
                    dve.wait_ge(slot_done.sem, slot_done.at(b, s + 1))
                    if HQ0 <= s < GZ0:
                        n = s - HQ0
                        dve.wait_ge(hq_sig.sem, hq_sig.at(b, n + 1))
                        V.scalar_tensor_tensor(out=q_h[:, n, :], in0=F[n % 2][:, :], scalar=float(P) ** -0.5,
                                               in1=gates[:, 0, n % 2, :], op0=ALU.mult,
                                               op1=ALU.mult).then_inc(hq_used.sem, 1)
                    if s in UP_SLOT:
                        j = UP_SLOT[s]
                        dve.wait_ge(mg_used.sem, mg_used.at(b, 2 * j + 2))
                        for g in range(2):
                            ins = V.tensor_tensor(gates[:, j % 2, g, :], gates[:, j % 2, g, :],
                                                  A[2 * (j % 2) + g][:, :], ALU.mult)
                            if g:
                                link(ins)
                        V.tensor_tensor(gates[:, j % 2, 0, :], gates[:, j % 2, 0, :], gates[:, j % 2, 1, :],
                                        ALU.add).then_inc(up_used.sem, 1)
                    if not (last and s + RING >= SLOTS):
                        split_lo(b if s + RING < SLOTS else b + 1, (s + RING) % SLOTS)
                    if s in UP_SLOT:
                        dve.wait_ge(m_hi_done.sem, m_hi_done.at(b, j + 1))
                        V.tensor_tensor(m_lo[:, j, :], gates[:, j % 2, 0, :], m_hi[:, j, :].bitcast(fp32),
                                        ALU.subtract).then_inc(m_split.sem, 1)
                    if s == 6:
                        dve.wait_ge(f_act.sem, f_act.at(b, 1))
                        V.scalar_tensor_tensor(out=pk[:, :, :], in0=z_f[:, :, :], scalar=0.0, in1=t1[:, :, :],
                                               op0=ALU.max, op1=ALU.add)
                        link(V.scalar_tensor_tensor(out=z_f[:, :, :], in0=z_f[:, :, :], scalar=0.0,
                                                    in1=t1[:, :, :], op0=ALU.min, op1=ALU.subtract))
                    if s == 7:
                        link(V.tensor_tensor(z_f[:, :, :], z_f[:, :, :], over_tiles(c2, 512), ALU.add))
                    if s == 8:
                        V.tensor_tensor(t1[:, :, :], z_f[:, :, :], over_tiles(c1, 512),
                                        ALU.subtract).then_inc(f_dve.sem, 1)
                        link(V.tensor_tensor(z_f[:, :, :], z_f[:, :, :], over_tiles(c1, 512), ALU.max))
                    if s == 11:
                        dve.wait_ge(f_act.sem, f_act.at(b, 2))
                        V.tensor_tensor(z_f[:, :, :], z_f[:, :, :], t1[:, :, :],
                                        ALU.add).then_inc(log_f_ready.sem, 1)
                    if s == 9:
                        dve.wait_ge(y_done.sem, y_done.at(b, 1))
                        for n in range(2):
                            ins = V.tensor_tensor(y_g[:, 2 * n:2 * n + 2, :],
                                                  R[n][:, :].rearrange("p (t n) -> p t n", t=2),
                                                  ba_bc.unsqueeze(1).broadcast_to([P, 2, GKW]), ALU.add)
                        ins.then_inc(y_added.sem, 1)
                    if s == 12:
                        dve.wait_ge(g_act.sem, g_act.at(b, 1))
                        V.scalar_tensor_tensor(out=y_g[:, :, :], in0=y_g[:, :, :], scalar=0.0, in1=t3[:, :, :],
                                               op0=ALU.min, op1=ALU.subtract).then_inc(log_a_ready.sem, 1)
                    if s in (13, 14):
                        for t in (0, 1) if s == 13 else (2, 3):
                            dve.wait_ge(grev_h_done.sem, grev_h_done.at(b, t + 1))
                            V.tensor_tensor(pk[:, t, :], R[t % 2][:, :], pk[:, t, :],
                                            ALU.subtract).then_inc(grev_h_used.sem, 1)
                    if s == 15:
                        dve.wait_ge(kexp_g.sem, kexp_g.at(b, 2))
                        V.tensor_tensor(gklr[:, :, 0:GKW], gklr[:, :, 0:GKW], t3[:, :, :],
                                        ALU.mult).then_inc(kdec_g_ready.sem, 1)
                    if s == 16:
                        dve.wait_ge(kexp_h.sem, kexp_h.at(b, 1))
                        V.tensor_tensor(kdec_h[:, :, :], pk[:, :, :], over_tiles(c3, 512),
                                        ALU.mult).then_inc(kdec_h_ready.sem, 1)
                    if s == 18:
                        dve.wait_ge(aT_done.sem, aT_done.at(b, 1))
                        V.tensor_copy(a_cols[:, :, :], R[0][:, 0:6 * NC_BLK]
                                      .rearrange("p (i c) -> p i c", i=6)).then_inc(a_ready.sem, 1)
                        dve.wait_ge(a_ready.sem, a_ready.at(b, 1))
                    for i in range(8):
                        if s == STEP_AT[i]:
                            fam, t = divmod(i, 4)
                            dve.wait_ge(dS_done.sem, dS_done.at(b, i + 1))
                            for c in range(2):
                                n = 2 * t + c
                                for g in range(4):
                                    if fam == 0:
                                        p, r = divmod(g, 2)
                                        rows_ = slice(64 * r, 64 * r + 64)
                                        ins = V.scalar_tensor_tensor(
                                            out=S_g[rows_, c, p, r, :], in0=S_g[rows_, 1 - c, p, r, :],
                                            scalar=a_cols[rows_, 4 + p, n:n + 1],
                                            in1=R[c][rows_, p * 256 + r * P:p * 256 + (r + 1) * P],
                                            op0=ALU.mult, op1=ALU.add)
                                    else:
                                        ins = V.scalar_tensor_tensor(
                                            out=S_h[:, c, g, :], in0=S_h[:, 1 - c, g, :],
                                            scalar=a_cols[:, g, n:n + 1], in1=R[c][:, g * P:(g + 1) * P],
                                            op0=ALU.mult, op1=ALU.add)
                                if c == 0:
                                    link(ins)
                                else:
                                    ins.then_inc(S_ready.sem, 1)
                                    dve.wait_ge(S_ready.sem, S_ready.at(b, i + 1))
                        if s == STEP_AT[i] + 2:
                            fam, t = divmod(i, 4)
                            dve.wait_ge(o_sq.sem, o_sq.at(b, i + 1))
                            V.tensor_reduce(out=ssq[:, fam, 4 * t:4 * t + 4], in_=h_tmp[:, 0:4, :],
                                            axis=AX.X, op=ALU.add).then_inc(ssq_done.sem, 1)
                    for fam, at in ((0, GZ0 + 3), (1, HZ0 + 3)):
                        if s == at + 1:
                            dve.wait_ge(z_used.sem, z_used.at(b, 4 * fam + 4))
                            dve.wait_ge(rstd_ready.sem, rstd_ready.at(b, fam + 1))
                            o_fam = o_tm[:, :, fam * 512:(fam + 1) * 512]
                            for t in range(NT):
                                ins = V.tensor_tensor(
                                    o_fam[:, t, :].rearrange("p (h n) -> p h n", h=4),
                                    o_fam[:, t, :].rearrange("p (h n) -> p h n", h=4),
                                    rstd[:, fam, 4 * t:4 * t + 4].unsqueeze(2).broadcast_to([P, 4, P]), ALU.mult)
                            link(ins)
                            V.tensor_tensor(o_fam, o_fam, v_g[:, :, :], ALU.mult).then_inc(og_ready.sem, 1)
                    for i in range(8):
                        if s == (29, 29, 29, 29, 30, 30, 31, 31)[i]:
                            fam, t = divmod(i, 4)
                            dve.wait_ge(o_hi_done.sem, o_hi_done.at(b, i + 1))
                            src = A[t] if fam == 0 else R[t % 2]
                            for hh in range(1):
                                dst = o_hi[:, 4 * fam:4 * fam + 4, t * P:(t + 1) * P]
                                V.scalar_tensor_tensor(
                                    out=o_lo[:, 4 * fam:4 * fam + 4, t * P:(t + 1) * P],
                                    in0=src[:, :].rearrange("p (a n) -> p a n", a=4),
                                    scalar=nw[:, fam:fam + 1], in1=dst.bitcast(fp32),
                                    op0=ALU.mult, op1=ALU.subtract).then_inc(o_split.sem, 1)
                    if not last:
                        if s == 52:
                            x_norm(b + 1, 0)
                            x_norm(b + 1, 1)
                        if s == 54:
                            h_mod(b + 1, 0)
                            h_low(b + 1, 0)
                        if s == 55:
                            h_mod(b + 1, 1)
                            h_low(b + 1, 1)
                            x_norm(b + 1, 2)
                        if s == 56:
                            x_norm(b + 1, 3)
                        if s == 57:
                            h_mod(b + 1, 2)
                            h_low(b + 1, 2)
                        if s == 58:
                            h_mod(b + 1, 3)
                            h_low(b + 1, 3)
                    if s == 59:
                        for t in range(NT):
                            dve.wait_ge(y_rstd.sem, y_rstd.at(b, t + 1))
                            V.scalar_tensor_tensor(out=xy[:, t, :], in0=xy[:, t, :], scalar=y_rs[:, t:t + 1],
                                                   in1=fnw_bc[:, :], op0=ALU.mult,
                                                   op1=ALU.mult).then_inc(y_ready.sem, 1)
                assert last or link_at[1] == DVE_LINKS, f"DVE_LINKS {link_at[1]}"

            with dve.Fori(0, NB - 1) as b:
                body(b, False)
            body(NB - 1, True)

        @block.tensor
        def _(pe):
            mm, tr = nc.tensor.matmul, nc.tensor.transpose

            def x_transpose(nb, t):
                pe.wait_ge(x_normed.sem, x_normed.at(nb, t + 1))
                if t:
                    pe.wait_ge(h_affine.sem, h_affine.at(nb, t))
                for k in range(KT):
                    last = tr(R[k // 4][:, (k % 4) * P:(k % 4 + 1) * P], xn[:, t % 2, k * P:(k + 1) * P],
                              ident[:, :])
                last.then_inc(xT_done.sem, 1)

            pe.wait_ge(c_ready, 1)
            for n in range(6):
                pe.wait_ge(ada_in[n % 2], 16 * (n // 2 + 1))
                if n >= 4:
                    pe.wait_ge(ada_dve, n - 3)
                for k in range(KT):
                    last = mm(A[n % 4][:, :], c_act[:, k:k + 1].broadcast_to([P, P]), ada_w[:, n % 2, k, :],
                              start=(k == 0), stop=(k == KT - 1))
                last.then_inc(ada_pe, 1)
            pe.wait_ge(consts, 1)
            pe.wait_ge(ada_dve, 6)
            for k in range(2 * KT):
                dst = (A[0], A[1], F[0], F[1])[k // 4]
                last = tr(dst[:, (k % 4) * P:(k % 4 + 1) * P], mod_bc[:, k * P:(k + 1) * P], ident[:, :])
            last.then_inc(modT, 1)
            pe.wait_ge(mod_ready, 1)
            for t in range(NT):
                x_transpose(0, t)

            PASSES = ((0, 0), (0, 1), (1, 0))
            h_, w_, o_, m_ = (h_hi, h_lo), (w_hi, w_lo), (o_hi, o_lo), (m_hi, m_lo)

            def token_major(b, s, part, parts, k_per, width, src, free, free_n, group):
                for t in range(NT):
                    if part == 0:
                        pe.wait_ge(free.sem, free.at(b, free_n + t))
                    for kk in range(k_per):
                        k = part * k_per + kk
                        for n, (ia, iw) in enumerate(PASSES):
                            last = mm(A[t][:, 0:width], src[ia][:, k, t * P:(t + 1) * P],
                                      w_[iw][:, s % RING, kk * width:(kk + 1) * width],
                                      start=(k == 0 and n == 0), stop=(k == KT - 1 and n == 2))
                    if t == NT - 1:
                        last.then_inc(slot_done.sem, 1)
                    elif part == parts - 1:
                        last.then_inc(a_done.sem, 1)

            def feature_major(b, s, dst):
                for k in range(KT):
                    for n, (iw, ia) in enumerate(PASSES):
                        last = mm(dst[:, :], w_[iw][:, s % RING, k * P:(k + 1) * P], h_[ia][:, k, :],
                                  start=(k == 0 and n == 0), stop=(k == KT - 1 and n == 2))
                last.then_inc(slot_done.sem, 1)

            def slot(b, s):
                if s == 18:
                    pe.wait_ge(a_rows_ready.sem, a_rows_ready.at(b, 2))
                pe.wait_ge(w_split.sem, w_split.at(b, s + 1))
                if s < GK0:
                    token_major(b, s, s - F0, 4, 2, 512, h_, out_used, -3, 0)
                elif s < I0:
                    token_major(b, s, s - GK0, 2, 4, GW, h_, f_copied, 1, 1)
                elif s < GV0:
                    token_major(b, s, s - I0, 4, 2, 512, h_, gk_copied, 1, 2)
                elif s < GQ0:
                    token_major(b, s, s - GV0, 4, 2, 512, h_, i_copied, 1, 3)
                elif s < HQ0:
                    n = s - GQ0
                    pe.wait_ge(mg_used.sem, mg_used.at(b, n - 1))
                    feature_major(b, s, F[n])
                elif s < GZ0:
                    n = s - HQ0
                    if n < 2:
                        pe.wait_ge(gq_used.sem, gq_used.at(b, n + 1))
                    else:
                        pe.wait_ge(hq_used.sem, hq_used.at(b, n - 1))
                    feature_major(b, s, F[n % 2])
                elif s < HZ0:
                    token_major(b, s, s - GZ0, 4, 2, 512, h_, gv_copied, 1, 4)
                elif s < MG0:
                    token_major(b, s, s - HZ0, 4, 2, 512, h_, z_used, 1, 5)
                elif s in MG_SLOT:
                    j, g = MG_SLOT[s]
                    if j == 0:
                        pe.wait_ge(o_copied.sem, o_copied.at(b, 7))
                    else:
                        pe.wait_ge(mg_used.sem, mg_used.at(b, 2 * j + g - 1))
                    feature_major(b, s, F[g])
                elif s in UP_SLOT:
                    j = UP_SLOT[s]
                    if j == 0:
                        pe.wait_ge(o_split.sem, o_split.at(b, 8))
                    elif j >= 2:
                        pe.wait_ge(up_used.sem, up_used.at(b, j - 1))
                    for g in range(2):
                        for k in range(HEADS):
                            for n, (iw, ia) in enumerate(PASSES):
                                kk = 4 * g + k
                                last = mm(A[2 * (j % 2) + g][:, :], w_[iw][:, s % RING, kk * P:(kk + 1) * P],
                                          o_[ia][:, kk, :], start=(k == 0 and n == 0),
                                          stop=(k == HEADS - 1 and n == 2))
                    last.then_inc(slot_done.sem, 1)
                else:
                    n, part = divmod(s - OUT0, 4)
                    if n == 0 and part == 0:
                        pe.wait_ge(m_split.sem, m_split.at(b, KT))
                        token_major(b, s, part, 4, 2, 512, m_, up_used, KT - 3, 6)
                    else:
                        token_major(b, s, part, 4, 2, 512, m_, out_used, 1, 7)

            def increments(b, i):
                fam, t = divmod(i, 4)
                if i == 0:
                    pe.wait_ge(a_ready.sem, a_ready.at(b, 1))
                    pe.wait_ge(kdec_g_ready.sem, kdec_g_ready.at(b, 1))
                if i == 4:
                    pe.wait_ge(kdec_h_ready.sem, kdec_h_ready.at(b, 1))
                for c in range(2):
                    fr = slice(c * CHUNK, (c + 1) * CHUNK)
                    if fam == 0:
                        for p in range(2):
                            last = mm(R[c][:, p * 256:(p + 1) * 256], gklr[fr, t, p * P:(p + 1) * P],
                                      v_g[fr, t, p * 256:(p + 1) * 256], start=True, stop=True)
                    else:
                        for g in range(4):
                            last = mm(R[c][:, g * P:(g + 1) * P], kdec_h[fr, t, g * P:(g + 1) * P],
                                      v_h[fr, t, g * P:(g + 1) * P], start=True, stop=True)
                last.then_inc(dS_done.sem, 1)

            def outputs(b, i):
                fam, t = divmod(i, 4)
                pe.wait_ge(S_ready.sem, S_ready.at(b, i + 1))
                if i == 0:
                    pe.wait_ge(hq_used.sem, hq_used.at(b, 4))
                elif i < 7:
                    pe.wait_ge(o_copied.sem, o_copied.at(b, i))
                dst = F[0] if i < 7 else R[0]
                for c in range(2):
                    fr = slice(t * P + c * CHUNK, t * P + (c + 1) * CHUNK)
                    if fam == 0:
                        for p in range(2):
                            last = mm(dst[c * CHUNK:(c + 1) * CHUNK, p * 256:(p + 1) * 256], q_g[:, p, fr],
                                      S_g[:, c, p, :, :].rearrange("p r n -> p (r n)"), start=True, stop=True)
                    else:
                        for g in range(4):
                            last = mm(dst[c * CHUNK:(c + 1) * CHUNK, g * P:(g + 1) * P], q_h[:, g, fr],
                                      S_h[:, c, g, :], start=True, stop=True)
                last.then_inc(o_done.sem, 1)

            def o_transpose(b, i):
                fam, t = divmod(i, 4)
                if t == 0:
                    pe.wait_ge(og_ready.sem, og_ready.at(b, fam + 1))
                if i == 0:
                    pe.wait_ge(z_used.sem, z_used.at(b, 8))
                if i == 4:
                    pe.wait_ge(o_copied.sem, o_copied.at(b, 8))
                if i >= 6:
                    pe.wait_ge(o_split.sem, o_split.at(b, i - 1))
                for g in range(4):
                    last = tr((A[t] if fam == 0 else R[t % 2])[:, g * P:(g + 1) * P],
                              o_tm[:, t, fam * 512 + g * P:fam * 512 + (g + 1) * P], ident[:, :])
                last.then_inc(oT_done.sem, 1)

            def hosted(b, s, last_block):
                if s == 6:
                    pe.wait_ge(gk_copied.sem, gk_copied.at(b, 4))
                    for t in range(NT):
                        last = tr(R[0][0:LR, t * P:(t + 1) * P], gklr[:, t, GKW:GW], ident[:, :])
                    last.then_inc(lrT_done.sem, 1)
                if s == 8:
                    pe.wait_ge(lrT_copied.sem, lrT_copied.at(b, 1))
                    for t in range(NT):
                        last = mm(R[t // 2][:, (t % 2) * GKW:(t % 2 + 1) * GKW], lrT[:, t * P:(t + 1) * P],
                                  wa2[:, :], start=True, stop=True)
                    last.then_inc(y_done.sem, 1)
                if s in (12, 13):
                    if s == 12:
                        pe.wait_ge(log_f_ready.sem, log_f_ready.at(b, 1))
                        pe.wait_ge(y_added.sem, y_added.at(b, 1))
                    for t in (0, 1) if s == 12 else (2, 3):
                        if t >= 2:
                            pe.wait_ge(grev_h_used.sem, grev_h_used.at(b, t - 1))
                        mm(R[t % 2][:, :], tri[:, 0, :], z_f[:, t, :], start=True,
                           stop=True).then_inc(grev_h_done.sem, 1)
                if s == 14:
                    pe.wait_ge(grev_h_used.sem, grev_h_used.at(b, 4))
                    pe.wait_ge(log_a_ready.sem, log_a_ready.at(b, 1))
                    for t in range(NT):
                        last = mm(R[t // 2][:, (t % 2) * GKW:(t % 2 + 1) * GKW], tri[:, 1, :], y_g[:, t, :],
                                  start=True, stop=True)
                    last.then_inc(grev_g_done.sem, 1)
                if s == 15:
                    pe.wait_ge(kexp_g.sem, kexp_g.at(b, 2))
                    for t in range(NT):
                        mm(R[0][0:NC_BLK, :], ind[:, 0, t, :], z_f[:, t, :], start=(t == 0), stop=(t == NT - 1))
                    for t in range(NT):
                        last = mm(R[1][0:NC_BLK, 0:GKW], ind[:, 1, t, :], y_g[:, t, :], start=(t == 0),
                                  stop=(t == NT - 1))
                    last.then_inc(gend_done.sem, 1)
                if s == 18:
                    for i in range(6):
                        last = tr(R[0][:, i * NC_BLK:(i + 1) * NC_BLK], a_rows[:, i * P:(i + 1) * P],
                                  ident[0:NC_BLK, 0:NC_BLK])
                    last.then_inc(aT_done.sem, 1)
                for i in range(8):
                    if s == STEP_AT[i] + 1:
                        outputs(b, i)
                    if s == STEP_AT[i]:
                        pass
                for i in range(8):
                    if s == STEP_AT[i]:
                        increments(b, i)
                if s == 28:
                    for i in range(4):
                        o_transpose(b, i)
                if s in (29, 30):
                    for i in (4, 5) if s == 29 else (6, 7):
                        o_transpose(b, i)
                if not last_block and s in XT_AT:
                    x_transpose(b + 1, XT_AT.index(s))

            def body(b, last):
                for s in range(SLOTS):
                    if s == 0:
                        pe.wait_ge(h_split.sem, h_split.at(b, NT))
                    slot(b, s)
                    hosted(b, s, last)

            with pe.Fori(0, NB - 1) as b:
                body(b, False)
            body(NB - 1, True)


def layout(np, inp):
    x = np.ascontiguousarray(inp["x"])
    n = x.shape[1]
    w = inp["w_in"][0]
    at, part = 0, {}
    for name, width in (("gq", 256), ("gk", 256), ("gv", 512), ("gz", 512), ("lr", 16), ("hq", 512),
                        ("hf", 512), ("hi", 512), ("hz", 512), ("mg", 2048)):
        part[name] = w[:, at:at + width]
        at += width
    stream = np.zeros((SLOTS, P, SLOT_W), w.dtype)

    def put(s, m):
        k = m.shape[0] // P
        stream[s, :, 0:k * m.shape[1]] = m.reshape(k, P, -1).transpose(1, 0, 2).reshape(P, -1)

    for s0, m, parts in ((F0, part["hf"], 4), (GK0, np.concatenate([part["gk"], part["lr"]], 1), 2),
                         (I0, part["hi"], 4), (GV0, part["gv"], 4), (GZ0, part["gz"], 4),
                         (HZ0, part["hz"], 4), (OUT0, inp["w_out"][0][:, 0:512], 4),
                         (OUT0 + 4, inp["w_out"][0][:, 512:1024], 4)):
        for i in range(parts):
            put(s0 + i, m[i * (D // parts):(i + 1) * (D // parts)])
    for i in range(2):
        put(GQ0 + i, part["gq"][:, i * P:(i + 1) * P])
    for i in range(4):
        put(HQ0 + i, part["hq"][:, i * P:(i + 1) * P])
    for s, (j, g) in MG_SLOT.items():
        put(s, part["mg"][:, g * D + j * P:g * D + (j + 1) * P])
    up = np.concatenate([inp["w_up_gla"][0], inp["w_up_hgrn"][0]], 0)
    for s, j in UP_SLOT.items():
        put(s, up[:, j * P:(j + 1) * P])

    def as_cols(v):
        return v.reshape(-1, P).T

    cols = np.concatenate([as_cols(inp["c"][0]), as_cols(inp["norm_w"][0]), as_cols(inp["merge_b"][0]),
                           as_cols(inp["gla_norm_w"][0]), as_cols(inp["hgrn_norm_w"][0])], 1)
    rows = np.concatenate([inp["hgrn_gamma"][0], inp["gla_ba"][0], inp["final_norm_w"], inp["ada_b"][0]])[None]
    ada = inp["ada_w"][0].reshape(KT, P, 6, 512).transpose(2, 1, 0, 3).reshape(6, P, KT * 512)
    return {"x": x.reshape(n, D), "wa2": inp["gla_wa2"][0], "cols": cols, "rows": rows,
            "w_stream": stream, "ada": ada}


def kernel(**inputs):
    import numpy as np
    import concourse.bacc as bacc
    from concourse.bass_utils import run_bass_kernel_spmd

    inp = {k: np.asarray(v) for k, v in inputs.items()}
    nc = bacc.Bacc("TRN2", target_bir_lowering=False, num_devices=1)
    arrays, aps = {}, {}
    for name, a in layout(np, inp).items():
        a = np.ascontiguousarray(a)
        arrays[f"in_{name}"] = a
        aps[name] = nc.dram_tensor(f"in_{name}", a.shape, mybir.dt.from_np(a.dtype), kind="ExternalInput").ap()
    out = nc.dram_tensor("result", list(aps["x"].shape), mybir.dt.float32, kind="ExternalOutput").ap()
    build(nc, aps["x"], aps["wa2"], aps["cols"], aps["rows"], aps["w_stream"], aps["ada"], out)
    r = run_bass_kernel_spmd(nc, [arrays], core_ids=[0])
    return r.results[0]["result"].reshape(inp["x"].shape)
```

```python
import concourse.bass as bass
from concourse import mybir
from contextlib import ExitStack

P = 128
D = 1024
KT = D // P
T = 512
NT = T // P
CHUNK = 64
NC_BLK = T // CHUNK
LR = 16
GKW = 256
GW = GKW + LR
HEADS = 4
EPS = 1e-6
RAW, RING = 4, 3
SLOT_W = 4 * GW

F0, GK0, I0, GV0, GQ0, HQ0, GZ0, HZ0, MG0 = 0, 4, 6, 10, 14, 16, 20, 24, 28
MG_SLOT, UP_SLOT, _s = {}, {}, MG0
for _j in range(KT):
    for _g in range(2):
        MG_SLOT[_s] = (_j, _g)
        _s += 1
    if _j >= 1:
        UP_SLOT[_s] = _j - 1
        _s += 1
UP_SLOT[_s] = KT - 1
_s += 1
OUT0 = _s
SLOTS = OUT0 + 8
UP_AT = {j: s for s, j in UP_SLOT.items()}
MG_AT = {v: s for s, v in MG_SLOT.items()}
STEP_AT = [GZ0 + i for i in range(8)]
OG_AT = [24, 24, 25, 26, 28, 28, 29, 29]
XT_AT = [50, 51, 53, 55]
assert SLOTS == 60 and SLOTS % RAW == 0 and SLOTS % RING == 0

ACT_LINKS, DVE_LINKS = 14, 23


def slot_width(s):
    return SLOT_W if GK0 <= s < I0 else 1024


class Signal:

    def __init__(self, sem, per, head=0):
        self.sem, self.per, self.head = sem, per, head

    def at(self, b, n):
        return b * self.per + (self.head + n)


def build(nc, x, mod_in, cols, rows, w_stream, ada, out):
    fp32, f32r = mybir.dt.float32, mybir.dt.float32r
    ALU, ACT, AX = mybir.AluOpType, mybir.ActivationFunctionType, mybir.AxisListType
    NB = x.shape[0] // T

    ctx = ExitStack()
    with ctx:
        base = nc.sbuf_base
        top = [(base + 31) // 32 * 32]

        def sb(name, shape, dt, at=None):
            size = 4
            for n in shape[1:]:
                size *= n
            if at is None:
                at = top[0]
                top[0] = (at + size + 31) // 32 * 32
            return nc.alloc_sbuf_tensor_at(name, shape, dt, offset=at)

        def here():
            return top[0]

        def sem(name):
            return ctx.enter_context(nc.semaphore(name))

        def signal(name, per, head=0):
            return Signal(sem(name), per, head)

        h_at = here()
        h_hi = sb("h_hi", [P, KT, T], f32r)
        h_lo = sb("h_lo", [P, KT, T], f32r)
        w_raw = sb("w_raw", [P, RAW, SLOT_W], fp32)
        w_hi = sb("w_hi", [P, RING, SLOT_W], f32r)
        w_lo = sb("w_lo", [P, RING, SLOT_W], f32r)
        o_at = here()
        o_hi = sb("o_hi", [P, 2 * HEADS, T], f32r)
        o_lo = sb("o_lo", [P, 2 * HEADS, T], f32r)
        z_f = sb("z_f", [P, NT, 512], fp32, at=o_at)
        t1 = sb("t1", [P, NT, 512], fp32, at=o_at + 8192)
        pk = sb("pk", [P, NT, 512], fp32, at=o_at + 16384)
        y_g = sb("y_g", [P, NT, GKW], fp32, at=o_at + 24576)
        t3 = sb("t3", [P, NT, GKW], fp32, at=o_at + 28672)
        lf_lo = sb("lf_lo", [P, NT, 512], f32r, at=o_at)
        lf_hi = sb("lf_hi", [P, NT, 512], f32r, at=o_at + 8192)
        la_lo = sb("la_lo", [P, NT, GKW], f32r, at=o_at + 24576)
        la_hi = sb("la_hi", [P, NT, GKW], f32r, at=o_at + 28672)
        ada_w = sb("ada_w", [P, 2, KT, 512], fp32, at=o_at)
        m_at = here()
        m_hi = sb("m_hi", [P, KT, T], f32r)
        m_lo = sb("m_lo", [P, KT, T], f32r)
        kdec_h = sb("kdec_h", [P, NT, 512], fp32, at=m_at)
        v_h = sb("v_h", [P, NT, 512], fp32, at=m_at + 8192)
        v_g = sb("v_g", [P, NT, 512], fp32, at=m_at + 16384)
        gklr = sb("gklr", [P, NT, GW], fp32, at=m_at + 24576)
        mod_bc = sb("mod_bc", [P, 3 * D], fp32, at=m_at)
        ada_b = sb("ada_b", [P, 3 * D], fp32, at=m_at + 12288)
        q_at = here()
        q_h = sb("q_h", [P, HEADS, T], fp32)
        xn = sb("xn", [P, 2, D], fp32, at=q_at)
        q_g = sb("q_g", [P, 2, T], fp32)
        oraw_at = here()
        o_tm = sb("o_tm", [P, NT, 2 * 512], fp32)
        xy = sb("xy", [P, NT, D], fp32, at=oraw_at)
        S_h = sb("S_h", [P, 2, HEADS, P], fp32)
        S_g = sb("S_g", [P, 2, 2, 2, P], fp32)
        a_cols = sb("a_cols", [P, 6, NC_BLK], fp32)
        gates_at = here()
        gates = sb("gates", [P, 2, 2, T], fp32)
        lrT = sb("lrT", [LR, T], fp32, at=gates_at)
        kexp = sb("kexp", [P, NT, GKW], fp32, at=gates_at + 4096)
        h_tmp_at = here()
        h_tmp = sb("h_tmp", [P, KT, P], fp32)
        a_rows = sb("a_rows", [NC_BLK, 768], fp32, at=h_tmp_at)
        row_bc = sb("row_bc", [P, 4, 512], fp32)
        c1, c2, c3 = row_bc[:, 0, :], row_bc[:, 1, :], row_bc[:, 2, :]
        ba_bc = row_bc[:, 3, 0:GKW]
        gate_bc = sb("gate_bc", [P, D], fp32)
        fnw_bc = sb("fnw_bc", [P, D], fp32)
        ident = sb("ident", [P, P], fp32)
        tri = sb("tri", [P, 2, P], f32r)
        ind = sb("ind", [P, 2, NT, NC_BLK], f32r)
        masks = sb("masks", [P, 2, P + NT * NC_BLK], fp32, at=h_at)
        wa2 = sb("wa2", [LR, GKW], fp32)
        n_cols = cols.shape[1]
        col = sb("col", [P, n_cols], fp32)
        cT, norm_w, merge_b, nw = col[:, 0:8], col[:, 8:16], col[:, 16:32], col[:, 32:34]
        a_col = sb("a_col", [P, KT], fp32)
        s_col = sb("s_col", [P, 2 * KT], fp32)
        small = sb("small", [P, 8], fp32)
        c_act = sb("c_act", [P, KT], fp32)
        mhalf = sb("mhalf", [P, 16], fp32)
        eps_t = sb("eps_t", [P, 16], fp32)
        ssq = sb("ssq", [P, 2, 16], fp32)
        rstd = sb("rstd", [P, 2, 16], fp32)
        x_ss = sb("x_ss", [P, NT], fp32)
        x_rs = sb("x_rs", [P, NT], fp32)
        y_ss = sb("y_ss", [P, NT], fp32)
        y_rs = sb("y_rs", [P, NT], fp32)
        assert top[0] <= nc.sbuf_usable_end, (top[0], nc.sbuf_usable_end)

        def bank(name):
            return ctx.enter_context(nc.psum_tensor(name, [P, 512], fp32))

        A = [bank(f"A{i}") for i in range(4)]
        F = [bank(f"F{i}") for i in range(2)]
        R = [bank(f"R{i}") for i in range(2)]
        O_BANK = [F[0], F[1], F[0], F[1], F[0], F[1], F[1], R[0]]

        raw_in = [signal(f"raw_in{r}", SLOTS // RAW * 16) for r in range(RAW)]
        w_hi_done = signal("w_hi_done", SLOTS)
        w_split = signal("w_split", SLOTS)
        slot_done = signal("slot_done", SLOTS)
        a_done = signal("a_done", 24)
        f_copied = signal("f_copied", 4)
        gk_copied = signal("gk_copied", 4)
        i_copied = signal("i_copied", 4)
        gv_copied = signal("gv_copied", 4)
        z_sig = signal("z_sig", 8)
        z_used = signal("z_used", 8)
        gq_used = signal("gq_used", 2)
        hq_sig = signal("hq_sig", 4)
        hq_used = signal("hq_used", 4)
        mg_used = signal("mg_used", 16, 16)
        up_used = signal("up_used", 8)
        m_hi_done = signal("m_hi_done", 8)
        m_split = signal("m_split", 8)
        out_used = signal("out_used", 8, 8)
        lrT_done, lrT_copied = signal("lrT_done", 1), signal("lrT_copied", 1)
        y_done, y_added = signal("y_done", 1), signal("y_added", 1)
        g_act = signal("g_act", 1)
        log_a_ready, la_hi_done, la_split = (signal("log_a_ready", 1), signal("la_hi_done", 1),
                                             signal("la_split", 1))
        f_act = signal("f_act", 2)
        f_dve = signal("f_dve", 1)
        log_f_ready, lf_hi_done, lf_split = (signal("log_f_ready", 1), signal("lf_hi_done", 1),
                                             signal("lf_split", 1))
        grev_h_done, grev_h_used = signal("grev_h_done", 4), signal("grev_h_used", 4)
        kexp_h = signal("kexp_h", 1)
        kdec_h_ready = signal("kdec_h_ready", 1)
        grev_g_done, kexp_g = signal("grev_g_done", 1), signal("kexp_g", 2)
        kdec_g_ready = signal("kdec_g_ready", 1)
        gend_done, a_rows_ready = signal("gend_done", 1), signal("a_rows_ready", 2)
        aT_done, a_ready = signal("aT_done", 1), signal("a_ready", 1)
        dS_done, S_ready = signal("dS_done", 8), signal("S_ready", 8)
        o_done, o_copied = signal("o_done", 8), signal("o_copied", 8)
        o_sq, ssq_done = signal("o_sq", 8), signal("ssq_done", 8)
        rstd_ready = signal("rstd_ready", 8)
        o_scaled, og_ready = signal("o_scaled", 8), signal("og_ready", 8)
        oT_done = signal("oT_done", 8)
        o_hi_done, o_split = signal("o_hi_done", 8), signal("o_split", 8)
        xn_in = [signal(f"xn_in{r}", 32) for r in range(2)]
        x_sq = signal("x_sq", 4)
        x_rstd = signal("x_rstd", 4)
        x_normed = signal("x_normed", 4)
        xT_done = signal("xT_done", 4)
        h_affine0, h_affine1 = signal("h_affine0", 4), signal("h_affine1", 4)
        h_hi_done, h_split = signal("h_hi_done", 4), signal("h_split", 4)
        xy_in = signal("xy_in", 16)
        y_sum = signal("y_sum", 4)
        y_sq, y_rstd, y_ready = signal("y_sq", 4), signal("y_rstd", 4), signal("y_ready", 4)
        out_stored = signal("out_stored", 64, 64)
        act_link, dve_link = sem("act_link"), sem("dve_link")
        const_in, pool_link, consts = sem("const_in"), sem("pool_link"), sem("consts")
        ada_in = [sem("ada_in0"), sem("ada_in1")]
        ada_pe, ada_dve, c_ready, modT, mod_ready = (sem("ada_pe"), sem("ada_dve"), sem("c_ready"),
                                                     sem("modT"), sem("mod_ready"))
        act_pre, dve_pre, pool_pow = sem("act_pre"), sem("dve_pre"), sem("pool_pow")

        def wait_tile(eng, b, group, t, s):
            if t < 3:
                eng.wait_ge(a_done.sem, a_done.at(b, 3 * group + t + 1))
            else:
                eng.wait_ge(slot_done.sem, slot_done.at(b, s + 1))

        block = ctx.enter_context(nc.Block())

        @block.sync
        def _(sp):
            def load_w(s):
                r = s % RAW
                sp.dma_start(w_raw[:, r, 0:slot_width(s)],
                             w_stream[s, :, 0:slot_width(s)]).then_inc(raw_in[r].sem, 16)

            def load_x(nb, t):
                sp.dma_start(xn[:, t % 2, :],
                             x[bass.ds(nb * T + t * P, P), :]).then_inc(xn_in[t % 2].sem, 16)

            sp.sem_inc(out_stored.sem, 64)
            sp.dma_start(col[:, :], cols[:, :]).then_inc(const_in, 16)
            sp.dma_start(row_bc[:, 0, :], rows[0:1, 0:512].partition_broadcast(P)
                         .rearrange("p a n -> p (a n)")).then_inc(const_in, 16)
            sp.dma_start(ba_bc, rows[0:1, 512:512 + GKW].partition_broadcast(P)
                         .rearrange("p a n -> p (a n)")).then_inc(const_in, 16)
            sp.dma_start(fnw_bc[:, :], rows[0:1, 768:768 + D].partition_broadcast(P)
                         .rearrange("p a n -> p (a n)")).then_inc(const_in, 16)
            sp.dma_start(ada_b[:, :], rows[0:1, 1792:1792 + 3 * D].partition_broadcast(P)
                         .rearrange("p a n -> p (a n)")).then_inc(const_in, 16)
            sp.dma_start(wa2[:, :], mod_in[:, :]).then_inc(const_in, 16)
            load_x(0, 0)
            load_x(0, 1)
            for n in range(6):
                if n >= 2:
                    sp.wait_ge(ada_pe, n - 1)
                sp.dma_start(ada_w[:, n % 2, :, :],
                             ada[n, :, :].rearrange("p (k n) -> p k n", k=KT)).then_inc(ada_in[n % 2], 16)
            for s in range(RAW):
                load_w(s)
            for t in (2, 3):
                sp.wait_ge(xT_done.sem, xT_done.at(0, t - 1))
                load_x(0, t)

            def body(b, last):
                for s in range(SLOTS):
                    if not (last and s + RAW >= SLOTS):
                        sp.wait_ge(w_split.sem, w_split.at(b, s + 1))
                        load_w((s + RAW) % SLOTS)
                    if s == 38:
                        sp.wait_ge(slot_done.sem, slot_done.at(b, UP_AT[0] + 1))
                        sp.dma_start(xy[:, :, :], x[bass.ds(b * T, T), :]
                                     .rearrange("(t p) d -> p t d", p=P)).then_inc(xy_in.sem, 16)
                    if s in (39, 40) and not last:
                        load_x(b + 1, s - 39)
                    if s in (52, 53) and not last:
                        sp.wait_ge(xT_done.sem, xT_done.at(b + 1, s - 51))
                        load_x(b + 1, s - 50)
                for t in range(NT):
                    sp.wait_ge(y_ready.sem, y_ready.at(b, t + 1))
                    sp.dma_start(out[bass.ds(b * T + t * P, P), :], xy[:, t, :]).then_inc(out_stored.sem, 16)

            with sp.Fori(0, NB - 1) as b:
                body(b, False)
            body(NB - 1, True)
            sp.wait_ge(out_stored.sem, out_stored.at(NB, 0))

        @block.gpsimd
        def _(pool):
            links = [0]

            def link(ins):
                links[0] += 1
                ins.then_inc(pool_link, 1)
                pool.wait_ge(pool_link, links[0])

            link(nc.gpsimd.memset(ident[:, :], 0.0))
            link(nc.gpsimd.affine_select(out=ident[:, :], in_=ident[:, :], compare_op=ALU.not_equal, fill=1.0,
                                         base=0, pattern=[[-1, P]], channel_multiplier=1))
            for v, val in ((0, 1.0), (1, 1.0 / 16.0)):
                link(nc.gpsimd.memset(masks[:, v, 0:P], val))
                link(nc.gpsimd.affine_select(out=masks[:, v, 0:P], in_=masks[:, v, 0:P], compare_op=ALU.is_gt,
                                             fill=0.0, base=0, pattern=[[-1, P]], channel_multiplier=1))
                link(nc.gpsimd.memset(masks[CHUNK:P, v, 0:CHUNK], 0.0))
                link(nc.gpsimd.memset(masks[:, v, P:P + NT * NC_BLK], 0.0))
                for t in range(NT):
                    for c in range(2):
                        at = P + t * NC_BLK + 2 * t + c
                        link(nc.gpsimd.memset(masks[c * CHUNK:(c + 1) * CHUNK, v, at:at + 1], val))
                link(nc.gpsimd.tensor_copy(tri[:, v, :], masks[:, v, 0:P]))
                link(nc.gpsimd.tensor_copy(ind[:, v, :, :].rearrange("p t c -> p (t c)"),
                                           masks[:, v, P:P + NT * NC_BLK]))
            link(nc.gpsimd.memset(mhalf[:, :], -0.5))
            link(nc.gpsimd.memset(eps_t[:, :], EPS))
            link(nc.gpsimd.memset(S_h[:, :, :, :], 0.0))
            nc.gpsimd.memset(S_g[:, :, :, :, :], 0.0).then_inc(consts, 1)

            pw = [0]

            def inverse_root(dst, src, ready):
                k = dst.shape[1]
                nc.gpsimd.tensor_tensor(dst, src, eps_t[:, 0:k], ALU.add).then_inc(pool_pow, 1)
                pw[0] += 1
                pool.wait_ge(pool_pow, pow_base(pw[0]))
                nc.gpsimd.tensor_tensor(dst, dst, mhalf[:, 0:k], ALU.pow).then_inc(ready.sem, 1)

            pow_base = lambda n: n

            def x_tile(nb, t):
                pool.wait_ge(x_sq.sem, x_sq.at(nb, t + 1))
                inverse_root(x_rs[:, t:t + 1], x_ss[:, t:t + 1], x_rstd)

            def h_low(nb, t):
                pool.wait_ge(h_hi_done.sem, h_hi_done.at(nb, t + 1))
                nc.gpsimd.tensor_tensor(h_lo[:, :, t * P:(t + 1) * P], h_tmp[:, :, :],
                                        h_hi[:, :, t * P:(t + 1) * P].bitcast(fp32),
                                        ALU.subtract).then_inc(h_split.sem, 1)

            x_tile(0, 0)
            x_tile(0, 1)
            for t in range(NT):
                if t >= 2:
                    x_tile(0, t)
                h_low(0, t)

            head = pw[0]
            PER = 8 + 2 * NT

            def body(b, last):
                nonlocal pow_base
                pw[0] = 0
                pow_base = lambda n: b * PER + (head + n)
                for i in range(8):
                    fam, t = divmod(i, 4)
                    pool.wait_ge(ssq_done.sem, ssq_done.at(b, i + 1))
                    inverse_root(rstd[:, fam, 4 * t:4 * t + 4], ssq[:, fam, 4 * t:4 * t + 4], rstd_ready)
                if not last:
                    x_tile(b + 1, 0)
                    x_tile(b + 1, 1)
                    h_low(b + 1, 0)
                    x_tile(b + 1, 2)
                    h_low(b + 1, 1)
                    x_tile(b + 1, 3)
                    h_low(b + 1, 2)
                    h_low(b + 1, 3)
                for t in range(NT):
                    pool.wait_ge(y_sq.sem, y_sq.at(b, t + 1))
                    inverse_root(y_rs[:, t:t + 1], y_ss[:, t:t + 1], y_rstd)

            with pool.Fori(0, NB - 1) as b:
                body(b, False)
            body(NB - 1, True)

        @block.scalar
        def _(act):
            AF = nc.scalar.activation
            link_at = [None, 0, 0]

            def link(ins):
                link_at[1] += 1
                ins.then_inc(act_link, 1)
                act.wait_ge(act_link, link_at[0] * ACT_LINKS + (link_at[2] + link_at[1])
                            if link_at[0] is not None else link_at[1])

            def split_hi(b, s):
                act.wait_ge(raw_in[s % RAW].sem, raw_in[s % RAW].at(b, (s // RAW + 1) * 16))
                n = slot_width(s)
                AF(w_hi[:, s % RING, 0:n], w_raw[:, s % RAW, 0:n], ACT.Copy).then_inc(w_hi_done.sem, 1)

            def x_square(nb, t):
                act.wait_ge(xn_in[t % 2].sem, xn_in[t % 2].at(nb, (t // 2 + 1) * 16))
                junk = h_tmp[:, :, :] if t < 2 else gates[:, 0, :, :]
                link(AF(junk.rearrange("p a n -> p (a n)"), xn[:, t % 2, :], ACT.Square, scale=D ** -0.5,
                        accum_out=x_ss[:, t:t + 1]))
                nc.scalar.activation(small[:, 0:1], x_ss[:, t:t + 1], ACT.Copy).then_inc(x_sq.sem, 1)

            def h_high(nb, t):
                act.wait_ge(xT_done.sem, xT_done.at(nb, t + 1))
                act.wait_ge(x_normed.sem, x_normed.at(nb, 2))
                if t:
                    act.wait_ge(h_split.sem, h_split.at(nb, t))
                for k in range(4, KT):
                    last = AF(h_tmp[:, k, :], R[1][:, (k % 4) * P:(k % 4 + 1) * P], ACT.Identity,
                              scale=a_col[:, k:k + 1], bias=s_col[:, k:k + 1])
                last.then_inc(h_affine1.sem, 1)
                act.wait_ge(h_affine1.sem, h_affine1.at(nb, t + 1))
                act.wait_ge(h_affine0.sem, h_affine0.at(nb, t + 1))
                AF(h_hi[:, :, t * P:(t + 1) * P], h_tmp[:, :, :], ACT.Copy).then_inc(h_hi_done.sem, 1)

            act.wait_ge(const_in, 96)
            link(AF(c_act[:, :], cT, ACT.Sigmoid))
            nc.scalar.activation(small[:, 0:1], c_act[:, 0:1], ACT.Copy).then_inc(act_pre, 1)
            for t in (0, 1):
                x_square(0, t)
            act.wait_ge(dve_pre, 1)
            AF(c2, c2, ACT.Exp).then_inc(act_pre, 1)
            act.wait_ge(dve_pre, 2)
            link(AF(c1, c1, ACT.Ln))
            AF(c2, c3, ACT.Ln).then_inc(act_pre, 1)
            for s in range(RING):
                split_hi(0, s)
            act.wait_ge(mod_ready, 1)
            for t in range(NT):
                if t >= 2:
                    if t == 3:
                        act.wait_ge(x_sq.sem, x_sq.at(0, 3))
                    x_square(0, t)
                h_high(0, t)
            link_at[2] = link_at[1]

            def softplus_abs(buf, signals):
                link(AF(buf, buf, ACT.Abs))
                link(AF(buf, buf, ACT.Exp, scale=-1.0))
                AF(buf, buf, ACT.Ln, bias=1.0).then_inc(signals.sem, 1)

            flat = lambda t: t[:, :, :].rearrange("p t n -> p (t n)")

            def body(b, last):
                link_at[0], link_at[1] = b, 0
                for s in range(SLOTS):
                    if s == F0 + 3:
                        for t in range(NT):
                            wait_tile(act, b, 0, t, s)
                            AF(z_f[:, t, :], A[t][:, :], ACT.Copy).then_inc(f_copied.sem, 1)
                    if s == GK0 + 1:
                        for t in range(NT):
                            wait_tile(act, b, 1, t, s)
                            AF(gklr[:, t, :], A[t][:, 0:GW], ACT.Copy).then_inc(gk_copied.sem, 1)
                    if s == I0 + 3:
                        for t in range(NT):
                            wait_tile(act, b, 2, t, s)
                            AF(v_h[:, t, :], A[t][:, :], ACT.Copy).then_inc(i_copied.sem, 1)
                    if s == GV0 + 3:
                        for t in range(NT):
                            wait_tile(act, b, 3, t, s)
                            AF(v_g[:, t, :], A[t][:, :], ACT.Copy).then_inc(gv_copied.sem, 1)
                    for fam, at in ((0, GZ0 + 3), (1, HZ0 + 3)):
                        if s == at:
                            if fam:
                                act.wait_ge(og_ready.sem, og_ready.at(b, 4))
                            for t in range(NT):
                                if fam == 0:
                                    act.wait_ge(dS_done.sem, dS_done.at(b, t + 1))
                                wait_tile(act, b, 4 + fam, t, s)
                                AF(v_g[:, t, :], A[t][:, :], ACT.Sigmoid).then_inc(z_sig.sem, 1)
                    act.wait_ge(slot_done.sem, slot_done.at(b, s + 1))
                    if GQ0 <= s < HQ0:
                        n = s - GQ0
                        AF(q_g[:, n, :], F[n % 2][:, :], ACT.Copy, scale=0.125).then_inc(gq_used.sem, 1)
                    if HQ0 <= s < GZ0:
                        n = s - HQ0
                        if n >= 2:
                            act.wait_ge(hq_used.sem, hq_used.at(b, n - 1))
                        AF(gates[:, 0, n % 2, :], F[n % 2][:, :], ACT.Sigmoid).then_inc(hq_sig.sem, 1)
                    if s in MG_SLOT:
                        j, g = MG_SLOT[s]
                        if j >= 2 and g == 0:
                            act.wait_ge(m_split.sem, m_split.at(b, j - 1))
                        AF(gates[:, j % 2, g, :], F[g][:, :], ACT.Sigmoid,
                           bias=merge_b[:, g * KT + j:g * KT + j + 1]).then_inc(mg_used.sem, 1)
                    if not (last and s + RING >= SLOTS):
                        split_hi(b if s + RING < SLOTS else b + 1, (s + RING) % SLOTS)
                    if s in UP_SLOT:
                        j = UP_SLOT[s]
                        act.wait_ge(up_used.sem, up_used.at(b, j + 1))
                        AF(m_hi[:, j, :], gates[:, j % 2, 0, :], ACT.Copy).then_inc(m_hi_done.sem, 1)
                    if s == 4:
                        act.wait_ge(f_copied.sem, f_copied.at(b, 4))
                        link(AF(flat(t1), flat(z_f), ACT.Abs))
                    if s == 5:
                        link(AF(flat(t1), flat(t1), ACT.Exp, scale=-1.0))
                        AF(flat(t1), flat(t1), ACT.Ln, bias=1.0).then_inc(f_act.sem, 1)
                    if s == 9:
                        act.wait_ge(f_dve.sem, f_dve.at(b, 1))
                        link(AF(flat(t1), flat(t1), ACT.Abs))
                    if s == 10:
                        link(AF(flat(t1), flat(t1), ACT.Exp, scale=-1.0))
                        AF(flat(t1), flat(t1), ACT.Ln, bias=1.0).then_inc(f_act.sem, 1)
                    if s == 7:
                        act.wait_ge(lrT_done.sem, lrT_done.at(b, 1))
                        AF(lrT[:, :], R[0][0:LR, :], ACT.Copy).then_inc(lrT_copied.sem, 1)
                    if s == 12:
                        act.wait_ge(log_f_ready.sem, log_f_ready.at(b, 1))
                        AF(flat(lf_hi), flat(z_f), ACT.Copy).then_inc(lf_hi_done.sem, 1)
                    if s == 13:
                        act.wait_ge(log_a_ready.sem, log_a_ready.at(b, 1))
                        AF(flat(la_hi), flat(y_g), ACT.Copy).then_inc(la_hi_done.sem, 1)
                    if s == 11:
                        act.wait_ge(y_added.sem, y_added.at(b, 1))
                        link(AF(flat(t3), flat(y_g), ACT.Abs))
                        link(AF(flat(t3), flat(t3), ACT.Exp, scale=-1.0))
                        AF(flat(t3), flat(t3), ACT.Ln, bias=1.0).then_inc(g_act.sem, 1)
                    if s == 16:
                        act.wait_ge(grev_h_used.sem, grev_h_used.at(b, 4))
                        AF(flat(pk), flat(pk), ACT.Exp).then_inc(kexp_h.sem, 1)
                        act.wait_ge(grev_g_done.sem, grev_g_done.at(b, 1))
                        for n in range(2):
                            AF(kexp[:, 2 * n:2 * n + 2, :].rearrange("p t n -> p (t n)"), R[n][:, :],
                               ACT.Exp).then_inc(kexp_g.sem, 1)
                    if s == 17:
                        act.wait_ge(gend_done.sem, gend_done.at(b, 1))
                        AF(a_rows[:, 0:512], R[0][0:NC_BLK, :], ACT.Exp).then_inc(a_rows_ready.sem, 1)
                        AF(a_rows[:, 512:768], R[1][0:NC_BLK, 0:GKW], ACT.Exp).then_inc(a_rows_ready.sem, 1)
                    for i in range(8):
                        if s == STEP_AT[i] + 1:
                            fam, t = divmod(i, 4)
                            if i == 0:
                                act.wait_ge(out_stored.sem, out_stored.at(b, 0))
                            act.wait_ge(o_done.sem, o_done.at(b, i + 1))
                            AF(o_tm[:, t, fam * 512:(fam + 1) * 512], O_BANK[i][:, :],
                               ACT.Copy).then_inc(o_copied.sem, 1)
                            act.wait_ge(o_copied.sem, o_copied.at(b, i + 1))
                            if i:
                                act.wait_ge(ssq_done.sem, ssq_done.at(b, i))
                            AF(h_tmp[:, 0:4, :].rearrange("p a n -> p (a n)"),
                               o_tm[:, t, fam * 512:(fam + 1) * 512], ACT.Square,
                               scale=P ** -0.5).then_inc(o_sq.sem, 1)
                    for i in range(8):
                        if s == (29, 29, 29, 29, 30, 30, 31, 31)[i]:
                            fam, t = divmod(i, 4)
                            act.wait_ge(oT_done.sem, oT_done.at(b, i + 1))
                            src = A[t] if fam == 0 else R[t % 2]
                            AF(o_hi[:, 4 * fam:4 * fam + 4, t * P:(t + 1) * P],
                               src[:, :].rearrange("p (a n) -> p a n", a=4), ACT.Copy,
                               scale=nw[:, fam:fam + 1]).then_inc(o_hi_done.sem, 1)
                    if not last:
                        if s == 42:
                            act.wait_ge(ssq_done.sem, ssq_done.at(b, 8))
                            x_square(b + 1, 0)
                            act.wait_ge(x_sq.sem, x_sq.at(b + 1, 1))
                            x_square(b + 1, 1)
                        if s in (51, 52, 54, 56):
                            h_high(b + 1, (51, 52, 54, 56).index(s))
                        if s == 52:
                            act.wait_ge(m_split.sem, m_split.at(b, 8))
                            x_square(b + 1, 2)
                        if s == 53:
                            act.wait_ge(x_sq.sem, x_sq.at(b + 1, 3))
                            x_square(b + 1, 3)
                    if s == 59:
                        for t in range(NT):
                            act.wait_ge(y_sum.sem, y_sum.at(b, t + 1))
                            link(AF(gates[:, 1, :, :].rearrange("p a n -> p (a n)"), xy[:, t, :], ACT.Square, scale=D ** -0.5,
                                    accum_out=y_ss[:, t:t + 1]))
                            nc.scalar.activation(small[:, 1:2], y_ss[:, t:t + 1], ACT.Copy).then_inc(y_sq.sem, 1)
                assert last or link_at[1] == ACT_LINKS, f"ACT_LINKS {link_at[1]}"

            with act.Fori(0, NB - 1) as b:
                body(b, False)
            body(NB - 1, True)

        @block.vector
        def _(dve):
            V = nc.vector
            link_at = [None, 0, 0]

            def link(ins):
                link_at[1] += 1
                ins.then_inc(dve_link, 1)
                dve.wait_ge(dve_link, link_at[0] * DVE_LINKS + (link_at[2] + link_at[1])
                            if link_at[0] is not None else link_at[1])

            def split_lo(b, s):
                dve.wait_ge(w_hi_done.sem, w_hi_done.at(b, s + 1))
                n = slot_width(s)
                V.tensor_tensor(w_lo[:, s % RING, 0:n], w_raw[:, s % RAW, 0:n],
                                w_hi[:, s % RING, 0:n].bitcast(fp32), ALU.subtract).then_inc(w_split.sem, 1)

            def x_norm(nb, t):
                dve.wait_ge(x_rstd.sem, x_rstd.at(nb, t + 1))
                V.tensor_scalar(xn[:, t % 2, :], xn[:, t % 2, :], x_rs[:, t:t + 1], None,
                                ALU.mult).then_inc(x_normed.sem, 1)

            def h_mod(nb, t):
                dve.wait_ge(xT_done.sem, xT_done.at(nb, t + 1))
                if t:
                    dve.wait_ge(h_split.sem, h_split.at(nb, t))
                for k in range(4):
                    last = V.tensor_scalar(h_tmp[:, k, :], R[0][:, k * P:(k + 1) * P],
                                           a_col[:, k:k + 1], s_col[:, k:k + 1], ALU.mult, ALU.add)
                last.then_inc(h_affine0.sem, 1)

            link(V.memset(small[:, 4:5], 0.0))
            dve.wait_ge(const_in, 96)
            dve.wait_ge(act_pre, 1)
            V.tensor_tensor(c_act[:, :], c_act[:, :], cT, ALU.mult).then_inc(c_ready, 1)
            V.tensor_tensor(c2, c1, c1, ALU.subtract).then_inc(dve_pre, 1)
            dve.wait_ge(act_pre, 2)
            link(V.reciprocal(c3, c2))
            link(V.tensor_tensor(c2, c2, c3, ALU.mult))
            link(V.tensor_tensor(c1, c2, c2, ALU.subtract))
            link(V.tensor_scalar(c1, c1, 0.0, 1.0 - 1e-6, ALU.max, ALU.min))
            link(V.tensor_scalar(c3, c1, -1.0, 1.0, ALU.mult, ALU.add))
            V.tensor_scalar(c1, c1, 1e-30, float(2 ** 50), ALU.max, ALU.mult).then_inc(dve_pre, 1)
            for t in (0, 1):
                x_norm(0, t)
            dve.wait_ge(act_pre, 3)
            link(V.tensor_scalar(c1, c1, -34.657359027997264, None, ALU.add))
            def modulation(n):
                dve.wait_ge(ada_pe, n + 1)
                V.tensor_tensor(mod_bc[:, n * 512:(n + 1) * 512], A[n % 4][:, :],
                                ada_b[:, n * 512:(n + 1) * 512], ALU.add).then_inc(ada_dve, 1)

            for n in range(4):
                modulation(n)
            dve.wait_ge(modT, 1)
            for g in range(4):
                src = (A[2], A[3], F[0], F[1])[g]
                link(V.tensor_copy(s_col[:, 4 * g:4 * g + 4], src[:, 0:512:P]))
            link(V.tensor_scalar(a_col[:, :], s_col[:, KT:2 * KT], 1.0, None, ALU.add))
            V.tensor_tensor(a_col[:, :], a_col[:, :], norm_w, ALU.mult).then_inc(mod_ready, 1)
            dve.wait_ge(mod_ready, 1)
            for s in range(RING):
                split_lo(0, s)
            for t in range(NT):
                if t >= 2:
                    x_norm(0, t)
                h_mod(0, t)
                if t in (1, 2):
                    modulation(t + 3)
            dve.wait_ge(ada_dve, 6)
            link(V.tensor_copy(gate_bc[:, :], mod_bc[:, 2 * D:3 * D]))
            link(V.memset(small[:, 5:6], 0.0))
            V.memset(small[:, 6:7], 0.0).then_inc(mg_used.sem, 16)
            V.memset(small[:, 7:8], 0.0).then_inc(out_used.sem, 8)
            link_at[2] = link_at[1]

            def over_tiles(row, n):
                return row.unsqueeze(1).broadcast_to([P, NT, n])

            def body(b, last):
                link_at[0], link_at[1] = b, 0
                for s in range(SLOTS):
                    if s in (GZ0 + 3, HZ0 + 3):
                        fam = (s - GZ0) // 4
                        for t in range(NT):
                            dve.wait_ge(z_sig.sem, z_sig.at(b, 4 * fam + t + 1))
                            V.tensor_tensor(v_g[:, t, :], A[t][:, :], v_g[:, t, :],
                                            ALU.mult).then_inc(z_used.sem, 1)
                    if s in (OUT0 + 3, OUT0 + 7):
                        n = (s - OUT0) // 4
                        if n == 0:
                            dve.wait_ge(xy_in.sem, xy_in.at(b, 16))
                        for t in range(NT):
                            wait_tile(dve, b, 6 + n, t, s)
                            cols_ = slice(n * 512, (n + 1) * 512)
                            y_tmp = q_g[:, t % 2, :]
                            V.tensor_tensor(y_tmp, A[t][:, :], gate_bc[:, cols_], ALU.mult).then_inc(out_used.sem, 1)
                            dve.wait_ge(out_used.sem, out_used.at(b, 4 * n + t + 1))
                            ins = V.tensor_tensor(xy[:, t, cols_], xy[:, t, cols_], y_tmp, ALU.add)
                            if n:
                                ins.then_inc(y_sum.sem, 1)
                            else:
                                link(ins)
                    dve.wait_ge(slot_done.sem, slot_done.at(b, s + 1))
                    if HQ0 <= s < GZ0:
                        n = s - HQ0
                        dve.wait_ge(hq_sig.sem, hq_sig.at(b, n + 1))
                        V.scalar_tensor_tensor(out=q_h[:, n, :], in0=F[n % 2][:, :], scalar=float(P) ** -0.5,
                                               in1=gates[:, 0, n % 2, :], op0=ALU.mult,
                                               op1=ALU.mult).then_inc(hq_used.sem, 1)
                    if s in UP_SLOT:
                        j = UP_SLOT[s]
                        dve.wait_ge(mg_used.sem, mg_used.at(b, 2 * j + 2))
                        for g in range(2):
                            ins = V.tensor_tensor(gates[:, j % 2, g, :], gates[:, j % 2, g, :],
                                                  A[2 * (j % 2) + g][:, :], ALU.mult)
                            if g:
                                link(ins)
                        V.tensor_tensor(gates[:, j % 2, 0, :], gates[:, j % 2, 0, :], gates[:, j % 2, 1, :],
                                        ALU.add).then_inc(up_used.sem, 1)
                    if not (last and s + RING >= SLOTS):
                        split_lo(b if s + RING < SLOTS else b + 1, (s + RING) % SLOTS)
                    if s in UP_SLOT:
                        dve.wait_ge(m_hi_done.sem, m_hi_done.at(b, j + 1))
                        V.tensor_tensor(m_lo[:, j, :], gates[:, j % 2, 0, :], m_hi[:, j, :].bitcast(fp32),
                                        ALU.subtract).then_inc(m_split.sem, 1)
                    if s == 6:
                        dve.wait_ge(f_act.sem, f_act.at(b, 1))
                        V.scalar_tensor_tensor(out=pk[:, :, :], in0=z_f[:, :, :], scalar=0.0, in1=t1[:, :, :],
                                               op0=ALU.max, op1=ALU.add)
                        link(V.scalar_tensor_tensor(out=z_f[:, :, :], in0=z_f[:, :, :], scalar=0.0,
                                                    in1=t1[:, :, :], op0=ALU.min, op1=ALU.subtract))
                    if s == 7:
                        link(V.tensor_tensor(z_f[:, :, :], z_f[:, :, :], over_tiles(c2, 512), ALU.add))
                    if s == 8:
                        V.tensor_tensor(t1[:, :, :], z_f[:, :, :], over_tiles(c1, 512),
                                        ALU.subtract).then_inc(f_dve.sem, 1)
                        link(V.tensor_tensor(z_f[:, :, :], z_f[:, :, :], over_tiles(c1, 512), ALU.max))
                    if s == 11:
                        dve.wait_ge(f_act.sem, f_act.at(b, 2))
                        V.tensor_tensor(z_f[:, :, :], z_f[:, :, :], t1[:, :, :],
                                        ALU.add).then_inc(log_f_ready.sem, 1)
                    if s == 12:
                        dve.wait_ge(lf_hi_done.sem, lf_hi_done.at(b, 1))
                        V.tensor_tensor(lf_lo[:, :, :], z_f[:, :, :], lf_hi[:, :, :].bitcast(fp32),
                                        ALU.subtract).then_inc(lf_split.sem, 1)
                    if s == 13:
                        dve.wait_ge(la_hi_done.sem, la_hi_done.at(b, 1))
                        V.tensor_tensor(la_lo[:, :, :], y_g[:, :, :], la_hi[:, :, :].bitcast(fp32),
                                        ALU.subtract).then_inc(la_split.sem, 1)
                    if s == 9:
                        dve.wait_ge(y_done.sem, y_done.at(b, 1))
                        for n in range(2):
                            ins = V.tensor_tensor(y_g[:, 2 * n:2 * n + 2, :],
                                                  R[n][:, :].rearrange("p (t n) -> p t n", t=2),
                                                  ba_bc.unsqueeze(1).broadcast_to([P, 2, GKW]), ALU.add)
                        ins.then_inc(y_added.sem, 1)
                    if s == 12:
                        dve.wait_ge(g_act.sem, g_act.at(b, 1))
                        V.scalar_tensor_tensor(out=y_g[:, :, :], in0=y_g[:, :, :], scalar=0.0, in1=t3[:, :, :],
                                               op0=ALU.min, op1=ALU.subtract).then_inc(log_a_ready.sem, 1)
                    if s in (14, 15):
                        for t in (0, 1) if s == 14 else (2, 3):
                            dve.wait_ge(grev_h_done.sem, grev_h_done.at(b, t + 1))
                            V.tensor_tensor(pk[:, t, :], R[t % 2][:, :], pk[:, t, :],
                                            ALU.subtract).then_inc(grev_h_used.sem, 1)
                    if s == 17:
                        dve.wait_ge(kexp_g.sem, kexp_g.at(b, 2))
                        V.tensor_tensor(gklr[:, :, 0:GKW], gklr[:, :, 0:GKW], kexp[:, :, :],
                                        ALU.mult).then_inc(kdec_g_ready.sem, 1)
                    if s == 18:
                        dve.wait_ge(kexp_h.sem, kexp_h.at(b, 1))
                        V.tensor_tensor(kdec_h[:, :, :], pk[:, :, :], over_tiles(c3, 512),
                                        ALU.mult).then_inc(kdec_h_ready.sem, 1)
                    if s == 19:
                        dve.wait_ge(aT_done.sem, aT_done.at(b, 1))
                        V.tensor_copy(a_cols[:, :, :], R[0][:, 0:6 * NC_BLK]
                                      .rearrange("p (i c) -> p i c", i=6)).then_inc(a_ready.sem, 1)
                        dve.wait_ge(a_ready.sem, a_ready.at(b, 1))
                    for i in range(8):
                        if s == STEP_AT[i]:
                            fam, t = divmod(i, 4)
                            dve.wait_ge(dS_done.sem, dS_done.at(b, i + 1))
                            for c in range(2):
                                n = 2 * t + c
                                for g in range(4):
                                    if fam == 0:
                                        p, r = divmod(g, 2)
                                        rows_ = slice(64 * r, 64 * r + 64)
                                        ins = V.scalar_tensor_tensor(
                                            out=S_g[rows_, c, p, r, :], in0=S_g[rows_, 1 - c, p, r, :],
                                            scalar=a_cols[rows_, 4 + p, n:n + 1],
                                            in1=R[c][rows_, p * 256 + r * P:p * 256 + (r + 1) * P],
                                            op0=ALU.mult, op1=ALU.add)
                                    else:
                                        ins = V.scalar_tensor_tensor(
                                            out=S_h[:, c, g, :], in0=S_h[:, 1 - c, g, :],
                                            scalar=a_cols[:, g, n:n + 1], in1=R[c][:, g * P:(g + 1) * P],
                                            op0=ALU.mult, op1=ALU.add)
                                if c == 0:
                                    link(ins)
                                else:
                                    ins.then_inc(S_ready.sem, 1)
                                    dve.wait_ge(S_ready.sem, S_ready.at(b, i + 1))
                    for i in range(8):
                        if s == STEP_AT[i] + 1:
                            fam, t = divmod(i, 4)
                            dve.wait_ge(o_sq.sem, o_sq.at(b, i + 1))
                            V.tensor_reduce(out=ssq[:, fam, 4 * t:4 * t + 4], in_=h_tmp[:, 0:4, :],
                                            axis=AX.X, op=ALU.add).then_inc(ssq_done.sem, 1)
                    for i in range(8):
                        fam, t = divmod(i, 4)
                        o_tile = o_tm[:, t, fam * 512:(fam + 1) * 512]
                        if s == STEP_AT[i] + 2:
                            dve.wait_ge(rstd_ready.sem, rstd_ready.at(b, i + 1))
                            heads = o_tile.rearrange("p (h n) -> p h n", h=HEADS)
                            V.tensor_tensor(heads, heads, rstd[:, fam, 4 * t:4 * t + 4].unsqueeze(2)
                                            .broadcast_to([P, HEADS, P]), ALU.mult).then_inc(o_scaled.sem, 1)
                        if s == OG_AT[i]:
                            dve.wait_ge(o_scaled.sem, o_scaled.at(b, i + 1))
                            dve.wait_ge(z_used.sem, z_used.at(b, i + 1))
                            V.tensor_tensor(o_tile, o_tile, v_g[:, t, :], ALU.mult).then_inc(og_ready.sem, 1)
                    for i in range(8):
                        if s == (29, 29, 29, 29, 30, 30, 31, 31)[i]:
                            fam, t = divmod(i, 4)
                            dve.wait_ge(o_hi_done.sem, o_hi_done.at(b, i + 1))
                            src = A[t] if fam == 0 else R[t % 2]
                            for hh in range(1):
                                dst = o_hi[:, 4 * fam:4 * fam + 4, t * P:(t + 1) * P]
                                V.scalar_tensor_tensor(
                                    out=o_lo[:, 4 * fam:4 * fam + 4, t * P:(t + 1) * P],
                                    in0=src[:, :].rearrange("p (a n) -> p a n", a=4),
                                    scalar=nw[:, fam:fam + 1], in1=dst.bitcast(fp32),
                                    op0=ALU.mult, op1=ALU.subtract).then_inc(o_split.sem, 1)
                    if not last:
                        if s == 43:
                            x_norm(b + 1, 0)
                            x_norm(b + 1, 1)
                        if s in (51, 52, 54, 56):
                            h_mod(b + 1, (51, 52, 54, 56).index(s))
                        if s in (53, 54):
                            x_norm(b + 1, s - 51)
                    if s == 59:
                        for t in range(NT):
                            dve.wait_ge(y_rstd.sem, y_rstd.at(b, t + 1))
                            V.scalar_tensor_tensor(out=xy[:, t, :], in0=xy[:, t, :], scalar=y_rs[:, t:t + 1],
                                                   in1=fnw_bc[:, :], op0=ALU.mult,
                                                   op1=ALU.mult).then_inc(y_ready.sem, 1)
                assert last or link_at[1] == DVE_LINKS, f"DVE_LINKS {link_at[1]}"

            with dve.Fori(0, NB - 1) as b:
                body(b, False)
            body(NB - 1, True)

        @block.tensor
        def _(pe):
            mm, tr = nc.tensor.matmul, nc.tensor.transpose

            def x_transpose(nb, t):
                pe.wait_ge(x_normed.sem, x_normed.at(nb, t + 1))
                if t:
                    pe.wait_ge(h_affine0.sem, h_affine0.at(nb, t))
                    pe.wait_ge(h_affine1.sem, h_affine1.at(nb, t))
                for k in range(KT):
                    last = tr(R[k // 4][:, (k % 4) * P:(k % 4 + 1) * P], xn[:, t % 2, k * P:(k + 1) * P],
                              ident[:, :])
                last.then_inc(xT_done.sem, 1)

            def modulation(n):
                pe.wait_ge(ada_in[n % 2], 16 * (n // 2 + 1))
                for k in range(KT):
                    last = mm(A[n % 4][:, :], c_act[:, k:k + 1].broadcast_to([P, P]), ada_w[:, n % 2, k, :],
                              start=(k == 0), stop=(k == KT - 1))
                last.then_inc(ada_pe, 1)

            pe.wait_ge(c_ready, 1)
            for n in range(4):
                modulation(n)
            pe.wait_ge(consts, 1)
            pe.wait_ge(ada_dve, 4)
            for k in range(2 * KT):
                dst = (A[2], A[3], F[0], F[1])[k // 4]
                last = tr(dst[:, (k % 4) * P:(k % 4 + 1) * P], mod_bc[:, k * P:(k + 1) * P], ident[:, :])
            last.then_inc(modT, 1)
            modulation(4)
            pe.wait_ge(mod_ready, 1)
            for t in range(NT):
                x_transpose(0, t)
                if t == 1:
                    modulation(5)

            PASSES = ((0, 0), (0, 1), (1, 0))
            h_, w_, o_, m_ = (h_hi, h_lo), (w_hi, w_lo), (o_hi, o_lo), (m_hi, m_lo)

            def token_major(b, s, part, parts, k_per, width, src, free, free_n=(1, 2, 3, 4)):
                for t in range(NT):
                    if part == 0:
                        pe.wait_ge(free.sem, free.at(b, free_n[t]))
                    for kk in range(k_per):
                        k = part * k_per + kk
                        for n, (ia, iw) in enumerate(PASSES):
                            last = mm(A[t][:, 0:width], src[ia][:, k, t * P:(t + 1) * P],
                                      w_[iw][:, s % RING, kk * width:(kk + 1) * width],
                                      start=(k == 0 and n == 0), stop=(k == KT - 1 and n == 2))
                    if t == NT - 1:
                        last.then_inc(slot_done.sem, 1)
                    elif part == parts - 1:
                        last.then_inc(a_done.sem, 1)

            def feature_major(b, s, dst):
                for k in range(KT):
                    for n, (iw, ia) in enumerate(PASSES):
                        last = mm(dst[:, :], w_[iw][:, s % RING, k * P:(k + 1) * P], h_[ia][:, k, :],
                                  start=(k == 0 and n == 0), stop=(k == KT - 1 and n == 2))
                last.then_inc(slot_done.sem, 1)

            def slot(b, s):
                if s == 19:
                    pe.wait_ge(a_rows_ready.sem, a_rows_ready.at(b, 2))
                pe.wait_ge(w_split.sem, w_split.at(b, s + 1))
                if s < GK0:
                    token_major(b, s, s - F0, 4, 2, 512, h_, out_used, (-3, -2, -1, 0))
                elif s < I0:
                    token_major(b, s, s - GK0, 2, 4, GW, h_, f_copied)
                elif s < GV0:
                    token_major(b, s, s - I0, 4, 2, 512, h_, gk_copied)
                elif s < GQ0:
                    token_major(b, s, s - GV0, 4, 2, 512, h_, i_copied)
                elif s < HQ0:
                    n = s - GQ0
                    pe.wait_ge(mg_used.sem, mg_used.at(b, n - 1))
                    feature_major(b, s, F[n])
                elif s < GZ0:
                    n = s - HQ0
                    if n < 2:
                        pe.wait_ge(gq_used.sem, gq_used.at(b, n + 1))
                    else:
                        pe.wait_ge(hq_used.sem, hq_used.at(b, n - 1))
                    feature_major(b, s, F[n % 2])
                elif s < HZ0:
                    token_major(b, s, s - GZ0, 4, 2, 512, h_, gv_copied)
                elif s < MG0:
                    token_major(b, s, s - HZ0, 4, 2, 512, h_, z_used)
                elif s in MG_SLOT:
                    j, g = MG_SLOT[s]
                    if j == 0:
                        pe.wait_ge(o_copied.sem, o_copied.at(b, (5, 7)[g]))
                    else:
                        pe.wait_ge(mg_used.sem, mg_used.at(b, 2 * j + g - 1))
                    feature_major(b, s, F[g])
                elif s in UP_SLOT:
                    j = UP_SLOT[s]
                    if j == 0:
                        pe.wait_ge(o_split.sem, o_split.at(b, 8))
                    elif j >= 2:
                        pe.wait_ge(up_used.sem, up_used.at(b, j - 1))
                    for g in range(2):
                        for k in range(HEADS):
                            for n, (iw, ia) in enumerate(PASSES):
                                kk = 4 * g + k
                                last = mm(A[2 * (j % 2) + g][:, :], w_[iw][:, s % RING, kk * P:(kk + 1) * P],
                                          o_[ia][:, kk, :], start=(k == 0 and n == 0),
                                          stop=(k == HEADS - 1 and n == 2))
                    last.then_inc(slot_done.sem, 1)
                else:
                    n, part = divmod(s - OUT0, 4)
                    if n == 0:
                        pe.wait_ge(m_split.sem, m_split.at(b, 2 * part + 2))
                        token_major(b, s, part, 4, 2, 512, m_, up_used, (7, 7, 8, 8))
                    else:
                        token_major(b, s, part, 4, 2, 512, m_, out_used)

            def increments(b, i):
                fam, t = divmod(i, 4)
                if i == 0:
                    pe.wait_ge(a_ready.sem, a_ready.at(b, 1))
                    pe.wait_ge(kdec_g_ready.sem, kdec_g_ready.at(b, 1))
                if i == 4:
                    pe.wait_ge(kdec_h_ready.sem, kdec_h_ready.at(b, 1))
                for c in range(2):
                    fr = slice(c * CHUNK, (c + 1) * CHUNK)
                    if fam == 0:
                        for p in range(2):
                            last = mm(R[c][:, p * 256:(p + 1) * 256], gklr[fr, t, p * P:(p + 1) * P],
                                      v_g[fr, t, p * 256:(p + 1) * 256], start=True, stop=True)
                    else:
                        for g in range(4):
                            last = mm(R[c][:, g * P:(g + 1) * P], kdec_h[fr, t, g * P:(g + 1) * P],
                                      v_h[fr, t, g * P:(g + 1) * P], start=True, stop=True)
                last.then_inc(dS_done.sem, 1)

            def outputs(b, i):
                fam, t = divmod(i, 4)
                pe.wait_ge(S_ready.sem, S_ready.at(b, i + 1))
                if i == 0:
                    pe.wait_ge(hq_used.sem, hq_used.at(b, 4))
                elif i < 7:
                    pe.wait_ge(o_copied.sem, o_copied.at(b, i if i == 6 else max(i - 1, 1)))
                dst = O_BANK[i]
                for c in range(2):
                    fr = slice(t * P + c * CHUNK, t * P + (c + 1) * CHUNK)
                    if fam == 0:
                        for p in range(2):
                            last = mm(dst[c * CHUNK:(c + 1) * CHUNK, p * 256:(p + 1) * 256], q_g[:, p, fr],
                                      S_g[:, c, p, :, :].rearrange("p r n -> p (r n)"), start=True, stop=True)
                    else:
                        for g in range(4):
                            last = mm(dst[c * CHUNK:(c + 1) * CHUNK, g * P:(g + 1) * P], q_h[:, g, fr],
                                      S_h[:, c, g, :], start=True, stop=True)
                last.then_inc(o_done.sem, 1)

            def o_transpose(b, i):
                fam, t = divmod(i, 4)
                pe.wait_ge(og_ready.sem, og_ready.at(b, i + 1))
                if i == 0:
                    pe.wait_ge(z_used.sem, z_used.at(b, 8))
                if i == 4:
                    pe.wait_ge(o_copied.sem, o_copied.at(b, 8))
                if i >= 6:
                    pe.wait_ge(o_split.sem, o_split.at(b, i - 1))
                for g in range(4):
                    last = tr((A[t] if fam == 0 else R[t % 2])[:, g * P:(g + 1) * P],
                              o_tm[:, t, fam * 512 + g * P:fam * 512 + (g + 1) * P], ident[:, :])
                last.then_inc(oT_done.sem, 1)

            def hosted(b, s, last_block):
                if s == 6:
                    pe.wait_ge(gk_copied.sem, gk_copied.at(b, 4))
                    for t in range(NT):
                        last = tr(R[0][0:LR, t * P:(t + 1) * P], gklr[:, t, GKW:GW], ident[:, :])
                    last.then_inc(lrT_done.sem, 1)
                if s == 8:
                    pe.wait_ge(lrT_copied.sem, lrT_copied.at(b, 1))
                    for t in range(NT):
                        last = mm(R[t // 2][:, (t % 2) * GKW:(t % 2 + 1) * GKW], lrT[:, t * P:(t + 1) * P],
                                  wa2[:, :], start=True, stop=True)
                    last.then_inc(y_done.sem, 1)
                if s in (14, 15):
                    if s == 14:
                        pe.wait_ge(lf_split.sem, lf_split.at(b, 1))
                        pe.wait_ge(y_added.sem, y_added.at(b, 1))
                    for t in (0, 1) if s == 14 else (2, 3):
                        if t >= 2:
                            pe.wait_ge(grev_h_used.sem, grev_h_used.at(b, t - 1))
                        mm(R[t % 2][:, :], tri[:, 0, :], lf_hi[:, t, :], start=True, stop=False)
                        mm(R[t % 2][:, :], tri[:, 0, :], lf_lo[:, t, :], start=False,
                           stop=True).then_inc(grev_h_done.sem, 1)
                if s == 16:
                    pe.wait_ge(grev_h_used.sem, grev_h_used.at(b, 4))
                    pe.wait_ge(la_split.sem, la_split.at(b, 1))
                    for t in range(NT):
                        dst = R[t // 2][:, (t % 2) * GKW:(t % 2 + 1) * GKW]
                        mm(dst, tri[:, 1, :], la_hi[:, t, :], start=True, stop=False)
                        last = mm(dst, tri[:, 1, :], la_lo[:, t, :], start=False, stop=True)
                    last.then_inc(grev_g_done.sem, 1)
                if s == 17:
                    pe.wait_ge(kexp_g.sem, kexp_g.at(b, 2))
                    for bank_, v, n, halves in ((R[0], 0, 512, (lf_hi, lf_lo)), (R[1], 1, GKW, (la_hi, la_lo))):
                        for t in range(NT):
                            for q, half in enumerate(halves):
                                last = mm(bank_[0:NC_BLK, 0:n], ind[:, v, t, :], half[:, t, :],
                                          start=(t == 0 and q == 0), stop=(t == NT - 1 and q == 1))
                    last.then_inc(gend_done.sem, 1)
                if s == 19:
                    for i in range(6):
                        last = tr(R[0][:, i * NC_BLK:(i + 1) * NC_BLK], a_rows[:, i * P:(i + 1) * P],
                                  ident[0:NC_BLK, 0:NC_BLK])
                    last.then_inc(aT_done.sem, 1)
                for i in range(8):
                    if s == STEP_AT[i] + 1:
                        outputs(b, i)
                    if s == STEP_AT[i]:
                        pass
                for i in range(8):
                    if s == STEP_AT[i]:
                        increments(b, i)
                if s == 28:
                    for i in range(4):
                        o_transpose(b, i)
                if s in (29, 30):
                    for i in (4, 5) if s == 29 else (6, 7):
                        o_transpose(b, i)
                if not last_block and s in XT_AT:
                    x_transpose(b + 1, XT_AT.index(s))

            def body(b, last):
                for s in range(SLOTS):
                    if s == 0:
                        pe.wait_ge(h_split.sem, h_split.at(b, NT))
                    slot(b, s)
                    hosted(b, s, last)

            with pe.Fori(0, NB - 1) as b:
                body(b, False)
            body(NB - 1, True)


def layout(np, inp):
    x = np.ascontiguousarray(inp["x"])
    n = x.shape[1]
    w = inp["w_in"][0]
    at, part = 0, {}
    for name, width in (("gq", 256), ("gk", 256), ("gv", 512), ("gz", 512), ("lr", 16), ("hq", 512),
                        ("hf", 512), ("hi", 512), ("hz", 512), ("mg", 2048)):
        part[name] = w[:, at:at + width]
        at += width
    stream = np.zeros((SLOTS, P, SLOT_W), w.dtype)

    def put(s, m):
        k = m.shape[0] // P
        stream[s, :, 0:k * m.shape[1]] = m.reshape(k, P, -1).transpose(1, 0, 2).reshape(P, -1)

    for s0, m, parts in ((F0, part["hf"], 4), (GK0, np.concatenate([part["gk"], part["lr"]], 1), 2),
                         (I0, part["hi"], 4), (GV0, part["gv"], 4), (GZ0, part["gz"], 4),
                         (HZ0, part["hz"], 4), (OUT0, inp["w_out"][0][:, 0:512], 4),
                         (OUT0 + 4, inp["w_out"][0][:, 512:1024], 4)):
        for i in range(parts):
            put(s0 + i, m[i * (D // parts):(i + 1) * (D // parts)])
    for i in range(2):
        put(GQ0 + i, part["gq"][:, i * P:(i + 1) * P])
    for i in range(4):
        put(HQ0 + i, part["hq"][:, i * P:(i + 1) * P])
    for s, (j, g) in MG_SLOT.items():
        put(s, part["mg"][:, g * D + j * P:g * D + (j + 1) * P])
    up = np.concatenate([inp["w_up_gla"][0], inp["w_up_hgrn"][0]], 0)
    for s, j in UP_SLOT.items():
        put(s, up[:, j * P:(j + 1) * P])

    def as_cols(v):
        return v.reshape(-1, P).T

    cols = np.concatenate([as_cols(inp["c"][0]), as_cols(inp["norm_w"][0]), as_cols(inp["merge_b"][0]),
                           as_cols(inp["gla_norm_w"][0]), as_cols(inp["hgrn_norm_w"][0])], 1)
    rows = np.concatenate([inp["hgrn_gamma"][0], inp["gla_ba"][0], inp["final_norm_w"], inp["ada_b"][0]])[None]
    ada = inp["ada_w"][0].reshape(KT, P, 6, 512).transpose(2, 1, 0, 3).reshape(6, P, KT * 512)
    return {"x": x.reshape(n, D), "wa2": inp["gla_wa2"][0], "cols": cols, "rows": rows,
            "w_stream": stream, "ada": ada}


def kernel(**inputs):
    import numpy as np
    import concourse.bacc as bacc
    from concourse.bass_utils import run_bass_kernel_spmd

    inp = {k: np.asarray(v) for k, v in inputs.items()}
    nc = bacc.Bacc("TRN2", target_bir_lowering=False, num_devices=1)
    arrays, aps = {}, {}
    for name, a in layout(np, inp).items():
        a = np.ascontiguousarray(a)
        arrays[f"in_{name}"] = a
        aps[name] = nc.dram_tensor(f"in_{name}", a.shape, mybir.dt.from_np(a.dtype), kind="ExternalInput").ap()
    out = nc.dram_tensor("result", list(aps["x"].shape), mybir.dt.float32, kind="ExternalOutput").ap()
    build(nc, aps["x"], aps["wa2"], aps["cols"], aps["rows"], aps["w_stream"], aps["ada"], out)
    r = run_bass_kernel_spmd(nc, [arrays], core_ids=[0])
    return r.results[0]["result"].reshape(inp["x"].shape)
```

```python
import concourse.bass as bass
from concourse import mybir
from contextlib import ExitStack

P = 128
D = 1024
KT = D // P
T = 512
NT = T // P
CHUNK = 64
NC_BLK = T // CHUNK
LR = 16
GKW = 256
GW = GKW + LR
HEADS = 4
EPS = 1e-6
RAW, RING = 4, 3
SLOT_W = 4 * GW

F0, GK0, I0, GV0, GQ0, HQ0, GZ0, HZ0, MG0 = 0, 4, 6, 10, 14, 16, 20, 24, 28
MG_SLOT, UP_SLOT, _s = {}, {}, MG0
for _j in range(KT):
    for _g in range(2):
        MG_SLOT[_s] = (_j, _g)
        _s += 1
    if _j >= 1:
        UP_SLOT[_s] = _j - 1
        _s += 1
UP_SLOT[_s] = KT - 1
_s += 1
OUT0 = _s
SLOTS = OUT0 + 8
UP_AT = {j: s for s, j in UP_SLOT.items()}
MG_AT = {v: s for s, v in MG_SLOT.items()}
STEP_AT = [GZ0 + i for i in range(8)]
OG_AT = [24, 24, 25, 26, 28, 28, 29, 29]
OT_AT = [28, 28, 28, 28, 29, 29, 30, 30]
XSQ_AT = [42, 42, 45, 46]
XR_AT = 48
XN_AT = [49, 51, 53, 56]
assert SLOTS == 60 and SLOTS % RAW == 0 and SLOTS % RING == 0

ADA_DVE = [5, 5, 6, 6, 3, 6]
ACT_LINKS, DVE_LINKS = 14, 23


def slot_width(s):
    return SLOT_W if GK0 <= s < I0 else 1024


class Signal:

    def __init__(self, sem, per, head=0):
        self.sem, self.per, self.head = sem, per, head

    def at(self, b, n):
        return b * self.per + (self.head + n)


def build(nc, x, xt, wa2_in, cols, rows, w_stream, ada, out):
    fp32, f32r = mybir.dt.float32, mybir.dt.float32r
    ALU, ACT, AX = mybir.AluOpType, mybir.ActivationFunctionType, mybir.AxisListType
    NB = x.shape[0] // T

    ctx = ExitStack()
    with ctx:
        base = nc.sbuf_base
        top = [(base + 31) // 32 * 32]

        def sb(name, shape, dt, at=None):
            size = 4
            for n in shape[1:]:
                size *= n
            if at is None:
                at = top[0]
                top[0] = (at + size + 31) // 32 * 32
            return nc.alloc_sbuf_tensor_at(name, shape, dt, offset=at)

        def here():
            return top[0]

        def sem(name):
            return ctx.enter_context(nc.semaphore(name))

        def signal(name, per, head=0):
            return Signal(sem(name), per, head)

        h_at = here()
        h_hi = sb("h_hi", [P, KT, T], f32r)
        h_lo = sb("h_lo", [P, KT, T], f32r)
        w_raw = sb("w_raw", [P, RAW, SLOT_W], fp32)
        w_hi = sb("w_hi", [P, RING, SLOT_W], f32r)
        w_lo = sb("w_lo", [P, RING, SLOT_W], f32r)
        o_at = here()
        o_hi = sb("o_hi", [P, 2 * HEADS, T], f32r)
        o_lo = sb("o_lo", [P, 2 * HEADS, T], f32r)
        z_f = sb("z_f", [P, NT, 512], fp32, at=o_at)
        t1 = sb("t1", [P, NT, 512], fp32, at=o_at + 8192)
        pk = sb("pk", [P, NT, 512], fp32, at=o_at + 16384)
        y_g = sb("y_g", [P, NT, GKW], fp32, at=o_at + 24576)
        t3 = sb("t3", [P, NT, GKW], fp32, at=o_at + 28672)
        lf_lo = sb("lf_lo", [P, NT, 512], f32r, at=o_at)
        lf_hi = sb("lf_hi", [P, NT, 512], f32r, at=o_at + 8192)
        la_lo = sb("la_lo", [P, NT, GKW], f32r, at=o_at + 24576)
        la_hi = sb("la_hi", [P, NT, GKW], f32r, at=o_at + 28672)
        m_at = here()
        m_hi = sb("m_hi", [P, KT, T], f32r)
        m_lo = sb("m_lo", [P, KT, T], f32r)
        kdec_h = sb("kdec_h", [P, NT, 512], fp32, at=m_at)
        v_h = sb("v_h", [P, NT, 512], fp32, at=m_at + 8192)
        v_g = sb("v_g", [P, NT, 512], fp32, at=m_at + 16384)
        gklr = sb("gklr", [P, NT, GW], fp32, at=m_at + 24576)
        ada_w = [sb(f"ada_w{n}", [P, KT, 512], fp32, at=at)
                 for n, at in enumerate((o_at, o_at + 16384, h_at + 16384, m_at + 16384))]
        mod_row = sb("mod_row", [P, 2 * D], fp32, at=m_at)
        gate_b = sb("gate_b", [P, D], fp32, at=m_at + 8192)
        q_at = here()
        q_h = sb("q_h", [P, HEADS, T], fp32)
        xn = sb("xn", [P, 2, D], fp32, at=q_at)
        xf = sb("xf", [P, 2, 2, T], fp32, at=q_at)
        q_g = sb("q_g", [P, 2, T], fp32)
        oraw_at = here()
        o_tm = sb("o_tm", [P, NT, 2 * 512], fp32)
        xy = sb("xy", [P, NT, D], fp32, at=oraw_at)
        S_h = sb("S_h", [P, 2, HEADS, P], fp32)
        S_g = sb("S_g", [P, 2, 2, 2, P], fp32)
        a_cols = sb("a_cols", [P, 6, NC_BLK], fp32)
        gates_at = here()
        gates = sb("gates", [P, 2, 2, T], fp32)
        lrT = sb("lrT", [LR, T], fp32, at=gates_at)
        kexp = sb("kexp", [P, NT, GKW], fp32, at=gates_at + 4096)
        h_tmp_at = here()
        h_tmp = sb("h_tmp", [P, KT, P], fp32)
        a_rows = sb("a_rows", [NC_BLK, 768], fp32, at=h_tmp_at)
        row_bc = sb("row_bc", [P, 4, 512], fp32)
        c1, c2, c3 = row_bc[:, 0, :], row_bc[:, 1, :], row_bc[:, 2, :]
        ba_bc = row_bc[:, 3, 0:GKW]
        gate_bc = sb("gate_bc", [P, D], fp32)
        fnw_bc = sb("fnw_bc", [P, D], fp32)
        ident = sb("ident", [P, P], fp32)
        tri = sb("tri", [P, 2, P], f32r)
        ind = sb("ind", [P, 2, NT, NC_BLK], f32r)
        masks = sb("masks", [P, 2, P + NT * NC_BLK], fp32, at=h_at)
        wa2 = sb("wa2", [LR, GKW], fp32)
        n_cols = cols.shape[1]
        col = sb("col", [P, n_cols], fp32)
        cT, norm_w, merge_b, nw = col[:, 0:8], col[:, 8:16], col[:, 16:32], col[:, 32:34]
        ada_b = col[:, 34:50]
        a_col = sb("a_col", [P, KT], fp32)
        s_col = sb("s_col", [P, 2 * KT], fp32)
        small = sb("small", [P, 8], fp32)
        c_act = sb("c_act", [P, KT], fp32)
        one = sb("one", [P, 1], fp32)
        mhalf = sb("mhalf", [P, 16], fp32)
        eps_t = sb("eps_t", [P, 16], fp32)
        ssq = sb("ssq", [P, 2, 16], fp32)
        rstd = sb("rstd", [P, 2, 16], fp32)
        x_ss = sb("x_ss", [P, NT], fp32)
        x_rs = sb("x_rs", [P, NT], fp32)
        y_ss = sb("y_ss", [P, NT], fp32)
        y_rs = sb("y_rs", [P, NT], fp32)
        assert top[0] <= nc.sbuf_usable_end, (top[0], nc.sbuf_usable_end)

        def bank(name):
            return ctx.enter_context(nc.psum_tensor(name, [P, 512], fp32))

        A = [bank(f"A{i}") for i in range(4)]
        F = [bank(f"F{i}") for i in range(2)]
        R = [bank(f"R{i}") for i in range(2)]
        O_BANK = [F[0], F[1], F[0], F[1], F[0], F[1], F[1], R[0]]
        OT_BANK = A + R + A[0:2]

        raw_in = [signal(f"raw_in{r}", SLOTS // RAW * 16) for r in range(RAW)]
        w_hi_done = signal("w_hi_done", SLOTS)
        w_split = signal("w_split", SLOTS)
        slot_done = signal("slot_done", SLOTS)
        a_done = signal("a_done", 24)
        f_copied = signal("f_copied", 4)
        gk_copied = signal("gk_copied", 4)
        i_copied = signal("i_copied", 4)
        gv_copied = signal("gv_copied", 4)
        z_sig = signal("z_sig", 8)
        z_used = signal("z_used", 8)
        gq_used = signal("gq_used", 2)
        hq_sig = signal("hq_sig", 4)
        hq_used = signal("hq_used", 4)
        mg_used = signal("mg_used", 16, 16)
        up_used = signal("up_used", 8)
        m_hi_done = signal("m_hi_done", 8)
        m_split = signal("m_split", 8)
        out_used = signal("out_used", 8, 8)
        lrT_done, lrT_copied = signal("lrT_done", 1), signal("lrT_copied", 1)
        y_done, y_added = signal("y_done", 1), signal("y_added", 1)
        g_act = signal("g_act", 1)
        log_a_ready, la_hi_done, la_split = (signal("log_a_ready", 1), signal("la_hi_done", 1),
                                             signal("la_split", 1))
        f_act = signal("f_act", 2)
        f_dve = signal("f_dve", 1)
        log_f_ready, lf_hi_done, lf_split = (signal("log_f_ready", 1), signal("lf_hi_done", 1),
                                             signal("lf_split", 1))
        grev_h_done, grev_h_used = signal("grev_h_done", 4), signal("grev_h_used", 4)
        kexp_h = signal("kexp_h", 1)
        kdec_h_ready = signal("kdec_h_ready", 1)
        grev_g_done, kexp_g = signal("grev_g_done", 1), signal("kexp_g", 2)
        kdec_g_ready = signal("kdec_g_ready", 1)
        gend_done, a_rows_ready = signal("gend_done", 1), signal("a_rows_ready", 2)
        aT_done, a_ready = signal("aT_done", 1), signal("a_ready", 1)
        dS_done, S_ready = signal("dS_done", 8), signal("S_ready", 8)
        o_done, o_copied = signal("o_done", 8), signal("o_copied", 8)
        o_sq, ssq_done = signal("o_sq", 8), signal("ssq_done", 8)
        rstd_ready = signal("rstd_ready", 8)
        o_scaled, og_ready = signal("o_scaled", 8), signal("og_ready", 8)
        oT_done = signal("oT_done", 8)
        o_hi_done, o_split = signal("o_hi_done", 8), signal("o_split", 8)
        xn_in = [signal(f"xn_in{r}", 32, -32) for r in range(2)]
        x_sq = signal("x_sq", 4)
        x_rstd = signal("x_rstd", 4)
        xf_in = [signal(f"xf_in{r}", 32, -32) for r in range(2)]
        x_diag, xr_done = signal("x_diag", 1), signal("xr_done", 1)
        x_scaled = signal("x_scaled", 4)
        h_hi_done, h_split = signal("h_hi_done", 4), signal("h_split", 4)
        xy_in = signal("xy_in", 16)
        y_sum = signal("y_sum", 4)
        y_sq, y_rstd, y_ready = signal("y_sq", 4), signal("y_rstd", 4), signal("y_ready", 4)
        out_stored = signal("out_stored", 64, 64)
        act_link, dve_link = sem("act_link"), sem("dve_link")
        const_in, pool_link, consts = sem("const_in"), sem("pool_link"), sem("consts")
        col_in, gamma_in, gate_b_in = sem("col_in"), sem("gamma_in"), sem("gate_b_in")
        first_x_in = [sem(f"first_x_in{t}") for t in range(NT)]
        first_xf_in = [sem(f"first_xf_in{j}") for j in range(4)]
        ada_in = [[sem(f"ada_in{n}{half}") for half in "ab"] for n in range(4)]
        ada_sum, ada_pe, mod_copied, modT, mod_col, c_ready, mod_ready = (
            sem("ada_sum"), sem("ada_pe"), sem("mod_copied"), sem("modT"), sem("mod_col"),
            sem("c_ready"), sem("mod_ready"))
        act_pre, dve_pre, pool_pow = sem("act_pre"), sem("dve_pre"), sem("pool_pow")

        def wait_tile(eng, b, group, t, s):
            if t < 3:
                eng.wait_ge(a_done.sem, a_done.at(b, 3 * group + t + 1))
            else:
                eng.wait_ge(slot_done.sem, slot_done.at(b, s + 1))

        def pair(j, first):
            return gates[:, j - 2, :, :] if first and j >= 2 else xf[:, j % 2, :, :]

        block = ctx.enter_context(nc.Block())

        @block.sync
        def _(sp):
            def load_w(s):
                r = s % RAW
                sp.dma_start(w_raw[:, r, 0:slot_width(s)],
                             w_stream[s, :, 0:slot_width(s)]).then_inc(raw_in[r].sem, 16)

            def load_x(nb, t):
                sp.dma_start(xn[:, t % 2, :],
                             x[bass.ds(nb * T + t * P, P), :]).then_inc(xn_in[t % 2].sem, 16)

            def load_first_x(t):
                sp.dma_start(xy[:, t, :], x[t * P:(t + 1) * P, :]).then_inc(first_x_in[t], 16)

            def load_pair(nb, j, first=False):
                sp.dma_start(pair(j, first), xt[bass.ds(nb * P, P), j * 2 * T:(j + 1) * 2 * T]
                             .rearrange("p (k n) -> p k n", k=2)).then_inc(
                                 first_xf_in[j] if first else xf_in[j % 2].sem, 16)

            def load_ada(n):
                for half in range(2):
                    ks = slice(4 * half, 4 * half + 4)
                    sp.dma_start(ada_w[n % 4][:, ks, :], ada[n, :, half * 2048:(half + 1) * 2048]
                                 .rearrange("p (k n) -> p k n", k=4)).then_inc(ada_in[n % 4][half], 16)

            def load_row(dst, at, signals=const_in):
                sp.dma_start(dst, rows[0:1, at:at + dst.shape[1]].partition_broadcast(P)
                             .rearrange("p a n -> p (a n)")).then_inc(signals, 16)

            sp.sem_inc(out_stored.sem, 64)
            sp.dma_start(col[:, :], cols[:, :]).then_inc(col_in, 16)
            load_ada(0)
            load_row(row_bc[:, 0, :], 0, gamma_in)
            load_ada(1)
            for t in range(NT):
                load_first_x(t)
            load_ada(2)
            load_ada(3)
            for j in (0, 1):
                load_pair(0, j, first=True)
            load_w(0)
            for n in (4, 5):
                sp.wait_ge(ada_pe, n - 3)
                load_ada(n)
            load_row(gate_b[:, :], 1792 + 2 * D, gate_b_in)
            for j in (2, 3):
                load_w(j - 1)
                load_pair(0, j, first=True)
            load_w(3)
            load_row(ba_bc, 512)
            load_row(fnw_bc[:, :], 768)
            sp.dma_start(wa2[:, :], wa2_in[:, :]).then_inc(const_in, 16)

            def body(b, last):
                for s in range(SLOTS):
                    if not (last and s + RAW >= SLOTS):
                        sp.wait_ge(w_split.sem, w_split.at(b, s + 1))
                        load_w((s + RAW) % SLOTS)
                    if s == 38:
                        sp.wait_ge(slot_done.sem, slot_done.at(b, UP_AT[0] + 1))
                        sp.dma_start(xy[:, :, :], x[bass.ds(b * T, T), :]
                                     .rearrange("(t p) d -> p t d", p=P)).then_inc(xy_in.sem, 16)
                    if s in (39, 40) and not last:
                        load_x(b + 1, s - 39)
                    if s == 45 and not last:
                        for t in (2, 3):
                            sp.wait_ge(x_sq.sem, x_sq.at(b + 1, t - 1))
                            load_x(b + 1, t)
                    if s in (50, 51) and not last:
                        sp.wait_ge(x_sq.sem, x_sq.at(b + 1, s - 47))
                        load_pair(b + 1, s - 50)
                    if s in (54, 56) and not last:
                        sp.wait_ge(h_split.sem, h_split.at(b + 1, (s - 52) // 2))
                        load_pair(b + 1, (s - 50) // 2)
                for t in range(NT):
                    sp.wait_ge(y_ready.sem, y_ready.at(b, t + 1))
                    sp.dma_start(out[bass.ds(b * T + t * P, P), :], xy[:, t, :]).then_inc(out_stored.sem, 16)

            with sp.Fori(0, NB - 1) as b:
                body(b, False)
            body(NB - 1, True)
            sp.wait_ge(out_stored.sem, out_stored.at(NB, 0))

        @block.gpsimd
        def _(pool):
            links = [0]

            def link(ins):
                links[0] += 1
                ins.then_inc(pool_link, 1)
                pool.wait_ge(pool_link, links[0])

            link(nc.gpsimd.memset(ident[:, :], 0.0))
            link(nc.gpsimd.affine_select(out=ident[:, :], in_=ident[:, :], compare_op=ALU.not_equal, fill=1.0,
                                         base=0, pattern=[[-1, P]], channel_multiplier=1))
            for v, val in ((0, 1.0), (1, 1.0 / 16.0)):
                link(nc.gpsimd.memset(masks[:, v, 0:P], val))
                link(nc.gpsimd.affine_select(out=masks[:, v, 0:P], in_=masks[:, v, 0:P], compare_op=ALU.is_gt,
                                             fill=0.0, base=0, pattern=[[-1, P]], channel_multiplier=1))
                link(nc.gpsimd.memset(masks[CHUNK:P, v, 0:CHUNK], 0.0))
                link(nc.gpsimd.memset(masks[:, v, P:P + NT * NC_BLK], 0.0))
                for t in range(NT):
                    for c in range(2):
                        at = P + t * NC_BLK + 2 * t + c
                        link(nc.gpsimd.memset(masks[c * CHUNK:(c + 1) * CHUNK, v, at:at + 1], val))
                link(nc.gpsimd.tensor_copy(tri[:, v, :], masks[:, v, 0:P]))
                link(nc.gpsimd.tensor_copy(ind[:, v, :, :].rearrange("p t c -> p (t c)"),
                                           masks[:, v, P:P + NT * NC_BLK]))
            link(nc.gpsimd.memset(mhalf[:, :], -0.5))
            link(nc.gpsimd.memset(eps_t[:, :], EPS))
            link(nc.gpsimd.memset(S_h[:, :, :, :], 0.0))
            nc.gpsimd.memset(S_g[:, :, :, :, :], 0.0).then_inc(consts, 1)

            pw = [0]

            def inverse_root(dst, src, ready):
                k = dst.shape[1]
                nc.gpsimd.tensor_tensor(dst, src, eps_t[:, 0:k], ALU.add).then_inc(pool_pow, 1)
                pw[0] += 1
                pool.wait_ge(pool_pow, pow_base(pw[0]))
                nc.gpsimd.tensor_tensor(dst, dst, mhalf[:, 0:k], ALU.pow).then_inc(ready.sem, 1)

            pow_base = lambda n: n

            def x_tile(nb, t):
                pool.wait_ge(x_sq.sem, x_sq.at(nb, t + 1))
                inverse_root(x_rs[:, t:t + 1], x_ss[:, t:t + 1], x_rstd)

            for t in range(NT):
                x_tile(0, t)

            head = pw[0]
            PER = 8 + 2 * NT

            def body(b, last):
                nonlocal pow_base
                pw[0] = 0
                pow_base = lambda n: b * PER + (head + n)
                for i in range(8):
                    fam, t = divmod(i, 4)
                    pool.wait_ge(ssq_done.sem, ssq_done.at(b, i + 1))
                    inverse_root(rstd[:, fam, 4 * t:4 * t + 4], ssq[:, fam, 4 * t:4 * t + 4], rstd_ready)
                if not last:
                    for t in range(NT):
                        x_tile(b + 1, t)
                for t in range(NT):
                    pool.wait_ge(y_sq.sem, y_sq.at(b, t + 1))
                    inverse_root(y_rs[:, t:t + 1], y_ss[:, t:t + 1], y_rstd)

            with pool.Fori(0, NB - 1) as b:
                body(b, False)
            body(NB - 1, True)

        @block.scalar
        def _(act):
            AF = nc.scalar.activation
            link_at = [None, 0, 0]

            def link(ins):
                link_at[1] += 1
                ins.then_inc(act_link, 1)
                act.wait_ge(act_link, link_at[0] * ACT_LINKS + (link_at[2] + link_at[1])
                            if link_at[0] is not None else link_at[1])

            def split_hi(b, s):
                act.wait_ge(raw_in[s % RAW].sem, raw_in[s % RAW].at(b, (s // RAW + 1) * 16))
                n = slot_width(s)
                AF(w_hi[:, s % RING, 0:n], w_raw[:, s % RAW, 0:n], ACT.Copy).then_inc(w_hi_done.sem, 1)

            def x_square(nb, t, first=False):
                if first:
                    act.wait_ge(first_x_in[t], 16)
                else:
                    act.wait_ge(xn_in[t % 2].sem, xn_in[t % 2].at(nb, (t // 2 + 1) * 16))
                if t:
                    act.wait_ge(x_sq.sem, x_sq.at(nb, t))
                link(AF(h_tmp[:, :, :].rearrange("p a n -> p (a n)"), xy[:, t, :] if first else xn[:, t % 2, :],
                        ACT.Square, scale=D ** -0.5, accum_out=x_ss[:, t:t + 1]))
                nc.scalar.activation(small[:, 0:1], x_ss[:, t:t + 1], ACT.Copy).then_inc(x_sq.sem, 1)

            def h_high(nb, j, first=False):
                act.wait_ge(x_scaled.sem, x_scaled.at(nb, j + 1))
                for kk in range(2):
                    k = 2 * j + kk
                    last = AF(h_hi[:, k, :], pair(j, first)[:, kk, :], ACT.Identity, bias=s_col[:, k:k + 1])
                last.then_inc(h_hi_done.sem, 1)

            act.wait_ge(col_in, 16)
            AF(c_act[:, :], cT, ACT.Sigmoid).then_inc(act_pre, 1)
            act.wait_ge(dve_pre, 1)
            AF(c2, c2, ACT.Exp).then_inc(act_pre, 1)
            for n in range(4):
                if n == 2:
                    for t in range(NT):
                        x_square(0, t, first=True)
                if n == 3:
                    act.wait_ge(dve_pre, 2)
                    link(AF(c1, c1, ACT.Ln))
                    AF(c2, c3, ACT.Ln).then_inc(act_pre, 1)
                act.wait_ge(ada_pe, n + 1)
                AF(mod_row[:, n * 512:(n + 1) * 512], A[n][:, :], ACT.Copy).then_inc(mod_copied, 1)
            act.wait_ge(mod_ready, 1)
            h_high(0, 0, first=True)
            split_hi(0, 0)
            h_high(0, 1, first=True)
            for s in range(1, RING):
                split_hi(0, s)
                h_high(0, s + 1, first=True)
            link_at[2] = link_at[1]

            def softplus_abs(buf, signals):
                link(AF(buf, buf, ACT.Abs))
                link(AF(buf, buf, ACT.Exp, scale=-1.0))
                AF(buf, buf, ACT.Ln, bias=1.0).then_inc(signals.sem, 1)

            flat = lambda t: t[:, :, :].rearrange("p t n -> p (t n)")

            def body(b, last):
                link_at[0], link_at[1] = b, 0
                for s in range(SLOTS):
                    if s == F0 + 3:
                        for t in range(NT):
                            wait_tile(act, b, 0, t, s)
                            AF(z_f[:, t, :], A[t][:, :], ACT.Copy).then_inc(f_copied.sem, 1)
                    if s == GK0 + 1:
                        for t in range(NT):
                            wait_tile(act, b, 1, t, s)
                            AF(gklr[:, t, :], A[t][:, 0:GW], ACT.Copy).then_inc(gk_copied.sem, 1)
                    if s == I0 + 3:
                        for t in range(NT):
                            wait_tile(act, b, 2, t, s)
                            AF(v_h[:, t, :], A[t][:, :], ACT.Copy).then_inc(i_copied.sem, 1)
                    if s == GV0 + 3:
                        for t in range(NT):
                            wait_tile(act, b, 3, t, s)
                            AF(v_g[:, t, :], A[t][:, :], ACT.Copy).then_inc(gv_copied.sem, 1)
                    for fam, at in ((0, GZ0 + 3), (1, HZ0 + 3)):
                        if s == at:
                            if fam:
                                act.wait_ge(og_ready.sem, og_ready.at(b, 4))
                            for t in range(NT):
                                if fam == 0:
                                    act.wait_ge(dS_done.sem, dS_done.at(b, t + 1))
                                wait_tile(act, b, 4 + fam, t, s)
                                AF(v_g[:, t, :], A[t][:, :], ACT.Sigmoid).then_inc(z_sig.sem, 1)
                    if s == SLOTS - 1:
                        for t in range(NT):
                            act.wait_ge(y_sum.sem, y_sum.at(b, t + 1))
                            link(AF(gates[:, 1, :, :].rearrange("p a n -> p (a n)"), xy[:, t, :], ACT.Square, scale=D ** -0.5,
                                    accum_out=y_ss[:, t:t + 1]))
                            nc.scalar.activation(small[:, 1:2], y_ss[:, t:t + 1], ACT.Copy).then_inc(y_sq.sem, 1)
                    act.wait_ge(slot_done.sem, slot_done.at(b, s + 1))
                    if GQ0 <= s < HQ0:
                        n = s - GQ0
                        AF(q_g[:, n, :], F[n % 2][:, :], ACT.Copy, scale=0.125).then_inc(gq_used.sem, 1)
                    if HQ0 <= s < GZ0:
                        n = s - HQ0
                        if n >= 2:
                            act.wait_ge(hq_used.sem, hq_used.at(b, n - 1))
                        AF(gates[:, 0, n % 2, :], F[n % 2][:, :], ACT.Sigmoid).then_inc(hq_sig.sem, 1)
                    if s in MG_SLOT:
                        j, g = MG_SLOT[s]
                        if j >= 2 and g == 0:
                            act.wait_ge(m_split.sem, m_split.at(b, j - 1))
                        AF(gates[:, j % 2, g, :], F[g][:, :], ACT.Sigmoid,
                           bias=merge_b[:, g * KT + j:g * KT + j + 1]).then_inc(mg_used.sem, 1)
                    if not (last and s + RING >= SLOTS):
                        split_hi(b if s + RING < SLOTS else b + 1, (s + RING) % SLOTS)
                    if s in UP_SLOT:
                        j = UP_SLOT[s]
                        act.wait_ge(up_used.sem, up_used.at(b, j + 1))
                        AF(m_hi[:, j, :], gates[:, j % 2, 0, :], ACT.Copy).then_inc(m_hi_done.sem, 1)
                    if s == 4:
                        act.wait_ge(f_copied.sem, f_copied.at(b, 4))
                        link(AF(flat(t1), flat(z_f), ACT.Abs))
                    if s == 5:
                        link(AF(flat(t1), flat(t1), ACT.Exp, scale=-1.0))
                        AF(flat(t1), flat(t1), ACT.Ln, bias=1.0).then_inc(f_act.sem, 1)
                    if s == 9:
                        act.wait_ge(f_dve.sem, f_dve.at(b, 1))
                        link(AF(flat(t1), flat(t1), ACT.Abs))
                    if s == 10:
                        link(AF(flat(t1), flat(t1), ACT.Exp, scale=-1.0))
                        AF(flat(t1), flat(t1), ACT.Ln, bias=1.0).then_inc(f_act.sem, 1)
                    if s == 7:
                        act.wait_ge(lrT_done.sem, lrT_done.at(b, 1))
                        AF(lrT[:, :], R[0][0:LR, :], ACT.Copy).then_inc(lrT_copied.sem, 1)
                    if s == 12:
                        act.wait_ge(log_f_ready.sem, log_f_ready.at(b, 1))
                        AF(flat(lf_hi), flat(z_f), ACT.Copy).then_inc(lf_hi_done.sem, 1)
                    if s == 13:
                        act.wait_ge(log_a_ready.sem, log_a_ready.at(b, 1))
                        AF(flat(la_hi), flat(y_g), ACT.Copy).then_inc(la_hi_done.sem, 1)
                    if s == 11:
                        act.wait_ge(y_added.sem, y_added.at(b, 1))
                        link(AF(flat(t3), flat(y_g), ACT.Abs))
                        link(AF(flat(t3), flat(t3), ACT.Exp, scale=-1.0))
                        AF(flat(t3), flat(t3), ACT.Ln, bias=1.0).then_inc(g_act.sem, 1)
                    if s == 16:
                        act.wait_ge(grev_h_used.sem, grev_h_used.at(b, 4))
                        AF(flat(pk), flat(pk), ACT.Exp).then_inc(kexp_h.sem, 1)
                        act.wait_ge(grev_g_done.sem, grev_g_done.at(b, 1))
                        for n in range(2):
                            AF(kexp[:, 2 * n:2 * n + 2, :].rearrange("p t n -> p (t n)"), R[n][:, :],
                               ACT.Exp).then_inc(kexp_g.sem, 1)
                    if s == 17:
                        act.wait_ge(gend_done.sem, gend_done.at(b, 1))
                        AF(a_rows[:, 0:512], R[0][0:NC_BLK, :], ACT.Exp).then_inc(a_rows_ready.sem, 1)
                        AF(a_rows[:, 512:768], R[1][0:NC_BLK, 0:GKW], ACT.Exp).then_inc(a_rows_ready.sem, 1)
                    for i in range(8):
                        if s == STEP_AT[i] + 1:
                            fam, t = divmod(i, 4)
                            if i == 0:
                                act.wait_ge(out_stored.sem, out_stored.at(b, 0))
                            act.wait_ge(o_done.sem, o_done.at(b, i + 1))
                            AF(o_tm[:, t, fam * 512:(fam + 1) * 512], O_BANK[i][:, :],
                               ACT.Copy).then_inc(o_copied.sem, 1)
                            act.wait_ge(o_copied.sem, o_copied.at(b, i + 1))
                            if i:
                                act.wait_ge(ssq_done.sem, ssq_done.at(b, i))
                            AF(h_tmp[:, 0:4, :].rearrange("p a n -> p (a n)"),
                               o_tm[:, t, fam * 512:(fam + 1) * 512], ACT.Square,
                               scale=P ** -0.5).then_inc(o_sq.sem, 1)
                    for i in range(8):
                        if s == OT_AT[i]:
                            fam, t = divmod(i, 4)
                            act.wait_ge(oT_done.sem, oT_done.at(b, i + 1))
                            AF(o_hi[:, 4 * fam:4 * fam + 4, t * P:(t + 1) * P],
                               OT_BANK[i][:, :].rearrange("p (a n) -> p a n", a=4), ACT.Copy,
                               scale=nw[:, fam:fam + 1]).then_inc(o_hi_done.sem, 1)
                    if not last:
                        for t in range(NT):
                            if s == XSQ_AT[t]:
                                if t == 0:
                                    act.wait_ge(ssq_done.sem, ssq_done.at(b, 8))
                                x_square(b + 1, t)
                        if s in XN_AT:
                            h_high(b + 1, XN_AT.index(s))
                assert last or link_at[1] == ACT_LINKS, f"ACT_LINKS {link_at[1]}"

            with act.Fori(0, NB - 1) as b:
                body(b, False)
            body(NB - 1, True)

        @block.vector
        def _(dve):
            V = nc.vector
            link_at = [None, 0, 0]

            def link(ins):
                link_at[1] += 1
                ins.then_inc(dve_link, 1)
                dve.wait_ge(dve_link, link_at[0] * DVE_LINKS + (link_at[2] + link_at[1])
                            if link_at[0] is not None else link_at[1])

            def split_lo(b, s):
                dve.wait_ge(w_hi_done.sem, w_hi_done.at(b, s + 1))
                n = slot_width(s)
                V.tensor_tensor(w_lo[:, s % RING, 0:n], w_raw[:, s % RAW, 0:n],
                                w_hi[:, s % RING, 0:n].bitcast(fp32), ALU.subtract).then_inc(w_split.sem, 1)

            def root_diagonals(nb):
                dve.wait_ge(x_rstd.sem, x_rstd.at(nb, NT))
                for t in range(NT):
                    last = V.tensor_scalar(h_tmp[:, t, :], ident[:, :], x_rs[:, t:t + 1], None, ALU.mult)
                last.then_inc(x_diag.sem, 1)

            def x_scale(nb, j, first=False):
                tiles = pair(j, first)
                dve.wait_ge(first_xf_in[j] if first else xf_in[j % 2].sem,
                            16 if first else xf_in[j % 2].at(nb, (j // 2 + 1) * 16))
                if j == 0:
                    dve.wait_ge(xr_done.sem, xr_done.at(nb, 1))
                for kk in range(2):
                    k = 2 * j + kk
                    last = V.scalar_tensor_tensor(out=tiles[:, kk, :], in0=tiles[:, kk, :],
                                                  scalar=a_col[:, k:k + 1], in1=R[0][:, :],
                                                  op0=ALU.mult, op1=ALU.mult)
                last.then_inc(x_scaled.sem, 1)

            def h_low(nb, j, first=False):
                dve.wait_ge(h_hi_done.sem, h_hi_done.at(nb, j + 1))
                dve.wait_ge(x_scaled.sem, x_scaled.at(nb, j + 1))
                for kk in range(2):
                    k = 2 * j + kk
                    last = V.scalar_tensor_tensor(out=h_lo[:, k, :], in0=pair(j, first)[:, kk, :],
                                                  scalar=s_col[:, k:k + 1], in1=h_hi[:, k, :].bitcast(fp32),
                                                  op0=ALU.add, op1=ALU.subtract)
                last.then_inc(h_split.sem, 1)

            def ada_partial(n):
                w = ada_w[n % 4]
                dve.wait_ge(ada_in[n % 4][0], 16 * (n // 4 + 1))
                for k in range(ADA_DVE[n]):
                    if k == 4:
                        dve.wait_ge(ada_in[n % 4][1], 16 * (n // 4 + 1))
                    if k == 0:
                        ins = V.tensor_scalar(w[:, 0, :], w[:, 0, :], c_act[:, 0:1], None, ALU.mult)
                    else:
                        ins = V.scalar_tensor_tensor(out=w[:, 0, :], in0=w[:, k, :], scalar=c_act[:, k:k + 1],
                                                     in1=w[:, 0, :], op0=ALU.mult, op1=ALU.add)
                    if k < ADA_DVE[n] - 1:
                        link(ins)
                ins.then_inc(ada_sum, 1)

            def mod_column(n):
                dve.wait_ge(modT, n + 1)
                V.tensor_tensor(s_col[:, 4 * n:4 * n + 4], F[n % 2][:, 0:512:P], ada_b[:, 4 * n:4 * n + 4],
                                ALU.add).then_inc(mod_col, 1)

            V.memset(one[:, :], 1.0)
            dve.wait_ge(col_in, 16)
            dve.wait_ge(act_pre, 1)
            link(V.tensor_tensor(c_act[:, :], c_act[:, :], cT, ALU.mult))
            V.memset(small[:, 4:5], 0.0).then_inc(c_ready, 1)
            ada_partial(0)
            dve.wait_ge(gamma_in, 16)
            V.tensor_tensor(c2, c1, c1, ALU.subtract).then_inc(dve_pre, 1)
            ada_partial(1)
            dve.wait_ge(act_pre, 2)
            link(V.reciprocal(c3, c2))
            link(V.tensor_tensor(c2, c2, c3, ALU.mult))
            link(V.tensor_tensor(c1, c2, c2, ALU.subtract))
            link(V.tensor_scalar(c1, c1, 0.0, 1.0 - 1e-6, ALU.max, ALU.min))
            link(V.tensor_scalar(c3, c1, -1.0, 1.0, ALU.mult, ALU.add))
            V.tensor_scalar(c1, c1, 1e-30, float(2 ** 50), ALU.max, ALU.mult).then_inc(dve_pre, 1)
            mod_column(0)
            ada_partial(2)
            dve.wait_ge(consts, 1)
            root_diagonals(0)
            ada_partial(3)
            mod_column(1)
            mod_column(2)
            mod_column(3)
            dve.wait_ge(mod_col, 4)
            link(V.tensor_scalar(a_col[:, :], s_col[:, KT:2 * KT], 1.0, None, ALU.add))
            V.tensor_tensor(a_col[:, :], a_col[:, :], norm_w, ALU.mult).then_inc(mod_ready, 1)
            dve.wait_ge(mod_ready, 1)
            x_scale(0, 0, first=True)
            x_scale(0, 1, first=True)
            h_low(0, 0, first=True)
            split_lo(0, 0)
            h_low(0, 1, first=True)
            ada_partial(4)
            ada_partial(5)
            V.memset(small[:, 7:8], 0.0).then_inc(out_used.sem, 6)
            dve.wait_ge(gate_b_in, 16)
            for n in range(2):
                dve.wait_ge(ada_pe, n + 5)
                cols_ = slice(n * 512, (n + 1) * 512)
                V.tensor_tensor(gate_bc[:, cols_], A[2 + n][:, :], gate_b[:, cols_], ALU.add).then_inc(out_used.sem, 1)
            dve.wait_ge(out_used.sem, 8)
            for s in range(1, RING):
                split_lo(0, s)
                x_scale(0, s + 1, first=True)
                h_low(0, s + 1, first=True)
            dve.wait_ge(const_in, 48)
            V.memset(small[:, 6:7], 0.0).then_inc(mg_used.sem, 16)
            dve.wait_ge(act_pre, 3)
            link(V.tensor_scalar(c1, c1, -34.657359027997264, None, ALU.add))
            link_at[2] = link_at[1]

            def over_tiles(row, n):
                return row.unsqueeze(1).broadcast_to([P, NT, n])

            def body(b, last):
                link_at[0], link_at[1] = b, 0
                for s in range(SLOTS):
                    if s in (GZ0 + 3, HZ0 + 3):
                        fam = (s - GZ0) // 4
                        for t in range(NT):
                            dve.wait_ge(z_sig.sem, z_sig.at(b, 4 * fam + t + 1))
                            V.tensor_tensor(v_g[:, t, :], A[t][:, :], v_g[:, t, :],
                                            ALU.mult).then_inc(z_used.sem, 1)
                    if s in (OUT0 + 3, OUT0 + 7):
                        n = (s - OUT0) // 4
                        if n == 0:
                            dve.wait_ge(xy_in.sem, xy_in.at(b, 16))
                        for t in range(NT):
                            wait_tile(dve, b, 6 + n, t, s)
                            cols_ = slice(n * 512, (n + 1) * 512)
                            y_tmp = q_g[:, t % 2, :]
                            V.tensor_tensor(y_tmp, A[t][:, :], gate_bc[:, cols_], ALU.mult).then_inc(out_used.sem, 1)
                            dve.wait_ge(out_used.sem, out_used.at(b, 4 * n + t + 1))
                            ins = V.tensor_tensor(xy[:, t, cols_], xy[:, t, cols_], y_tmp, ALU.add)
                            if n:
                                ins.then_inc(y_sum.sem, 1)
                            else:
                                link(ins)
                    dve.wait_ge(slot_done.sem, slot_done.at(b, s + 1))
                    if HQ0 <= s < GZ0:
                        n = s - HQ0
                        dve.wait_ge(hq_sig.sem, hq_sig.at(b, n + 1))
                        V.scalar_tensor_tensor(out=q_h[:, n, :], in0=F[n % 2][:, :], scalar=float(P) ** -0.5,
                                               in1=gates[:, 0, n % 2, :], op0=ALU.mult,
                                               op1=ALU.mult).then_inc(hq_used.sem, 1)
                    if s in UP_SLOT:
                        j = UP_SLOT[s]
                        dve.wait_ge(mg_used.sem, mg_used.at(b, 2 * j + 2))
                        for g in range(2):
                            ins = V.tensor_tensor(gates[:, j % 2, g, :], gates[:, j % 2, g, :],
                                                  A[2 * (j % 2) + g][:, :], ALU.mult)
                            if g:
                                link(ins)
                        V.tensor_tensor(gates[:, j % 2, 0, :], gates[:, j % 2, 0, :], gates[:, j % 2, 1, :],
                                        ALU.add).then_inc(up_used.sem, 1)
                    if not (last and s + RING >= SLOTS):
                        split_lo(b if s + RING < SLOTS else b + 1, (s + RING) % SLOTS)
                    if s in UP_SLOT:
                        dve.wait_ge(m_hi_done.sem, m_hi_done.at(b, j + 1))
                        V.tensor_tensor(m_lo[:, j, :], gates[:, j % 2, 0, :], m_hi[:, j, :].bitcast(fp32),
                                        ALU.subtract).then_inc(m_split.sem, 1)
                    if s == 6:
                        dve.wait_ge(f_act.sem, f_act.at(b, 1))
                        V.scalar_tensor_tensor(out=pk[:, :, :], in0=z_f[:, :, :], scalar=0.0, in1=t1[:, :, :],
                                               op0=ALU.max, op1=ALU.add)
                        link(V.scalar_tensor_tensor(out=z_f[:, :, :], in0=z_f[:, :, :], scalar=0.0,
                                                    in1=t1[:, :, :], op0=ALU.min, op1=ALU.subtract))
                    if s == 7:
                        link(V.tensor_tensor(z_f[:, :, :], z_f[:, :, :], over_tiles(c2, 512), ALU.add))
                    if s == 8:
                        V.tensor_tensor(t1[:, :, :], z_f[:, :, :], over_tiles(c1, 512),
                                        ALU.subtract).then_inc(f_dve.sem, 1)
                        link(V.tensor_tensor(z_f[:, :, :], z_f[:, :, :], over_tiles(c1, 512), ALU.max))
                    if s == 11:
                        dve.wait_ge(f_act.sem, f_act.at(b, 2))
                        V.tensor_tensor(z_f[:, :, :], z_f[:, :, :], t1[:, :, :],
                                        ALU.add).then_inc(log_f_ready.sem, 1)
                    if s == 12:
                        dve.wait_ge(lf_hi_done.sem, lf_hi_done.at(b, 1))
                        V.tensor_tensor(lf_lo[:, :, :], z_f[:, :, :], lf_hi[:, :, :].bitcast(fp32),
                                        ALU.subtract).then_inc(lf_split.sem, 1)
                    if s == 13:
                        dve.wait_ge(la_hi_done.sem, la_hi_done.at(b, 1))
                        V.tensor_tensor(la_lo[:, :, :], y_g[:, :, :], la_hi[:, :, :].bitcast(fp32),
                                        ALU.subtract).then_inc(la_split.sem, 1)
                    if s == 9:
                        dve.wait_ge(y_done.sem, y_done.at(b, 1))
                        for n in range(2):
                            ins = V.tensor_tensor(y_g[:, 2 * n:2 * n + 2, :],
                                                  R[n][:, :].rearrange("p (t n) -> p t n", t=2),
                                                  ba_bc.unsqueeze(1).broadcast_to([P, 2, GKW]), ALU.add)
                        ins.then_inc(y_added.sem, 1)
                    if s == 12:
                        dve.wait_ge(g_act.sem, g_act.at(b, 1))
                        V.scalar_tensor_tensor(out=y_g[:, :, :], in0=y_g[:, :, :], scalar=0.0, in1=t3[:, :, :],
                                               op0=ALU.min, op1=ALU.subtract).then_inc(log_a_ready.sem, 1)
                    if s in (14, 15):
                        for t in (0, 1) if s == 14 else (2, 3):
                            dve.wait_ge(grev_h_done.sem, grev_h_done.at(b, t + 1))
                            V.tensor_tensor(pk[:, t, :], R[t % 2][:, :], pk[:, t, :],
                                            ALU.subtract).then_inc(grev_h_used.sem, 1)
                    if s == 17:
                        dve.wait_ge(kexp_g.sem, kexp_g.at(b, 2))
                        V.tensor_tensor(gklr[:, :, 0:GKW], gklr[:, :, 0:GKW], kexp[:, :, :],
                                        ALU.mult).then_inc(kdec_g_ready.sem, 1)
                    if s == 18:
                        dve.wait_ge(kexp_h.sem, kexp_h.at(b, 1))
                        V.tensor_tensor(kdec_h[:, :, :], pk[:, :, :], over_tiles(c3, 512),
                                        ALU.mult).then_inc(kdec_h_ready.sem, 1)
                    if s == 19:
                        dve.wait_ge(aT_done.sem, aT_done.at(b, 1))
                        V.tensor_copy(a_cols[:, :, :], R[0][:, 0:6 * NC_BLK]
                                      .rearrange("p (i c) -> p i c", i=6)).then_inc(a_ready.sem, 1)
                        dve.wait_ge(a_ready.sem, a_ready.at(b, 1))
                    for i in range(8):
                        if s == STEP_AT[i]:
                            fam, t = divmod(i, 4)
                            dve.wait_ge(dS_done.sem, dS_done.at(b, i + 1))
                            for c in range(2):
                                n = 2 * t + c
                                for g in range(4):
                                    if fam == 0:
                                        p, r = divmod(g, 2)
                                        rows_ = slice(64 * r, 64 * r + 64)
                                        ins = V.scalar_tensor_tensor(
                                            out=S_g[rows_, c, p, r, :], in0=S_g[rows_, 1 - c, p, r, :],
                                            scalar=a_cols[rows_, 4 + p, n:n + 1],
                                            in1=R[c][rows_, p * 256 + r * P:p * 256 + (r + 1) * P],
                                            op0=ALU.mult, op1=ALU.add)
                                    else:
                                        ins = V.scalar_tensor_tensor(
                                            out=S_h[:, c, g, :], in0=S_h[:, 1 - c, g, :],
                                            scalar=a_cols[:, g, n:n + 1], in1=R[c][:, g * P:(g + 1) * P],
                                            op0=ALU.mult, op1=ALU.add)
                                if c == 0:
                                    link(ins)
                                else:
                                    ins.then_inc(S_ready.sem, 1)
                                    dve.wait_ge(S_ready.sem, S_ready.at(b, i + 1))
                    for i in range(8):
                        if s == STEP_AT[i] + 1:
                            fam, t = divmod(i, 4)
                            dve.wait_ge(o_sq.sem, o_sq.at(b, i + 1))
                            V.tensor_reduce(out=ssq[:, fam, 4 * t:4 * t + 4], in_=h_tmp[:, 0:4, :],
                                            axis=AX.X, op=ALU.add).then_inc(ssq_done.sem, 1)
                    for i in range(8):
                        fam, t = divmod(i, 4)
                        o_tile = o_tm[:, t, fam * 512:(fam + 1) * 512]
                        if s == STEP_AT[i] + 2:
                            dve.wait_ge(rstd_ready.sem, rstd_ready.at(b, i + 1))
                            heads = o_tile.rearrange("p (h n) -> p h n", h=HEADS)
                            V.tensor_tensor(heads, heads, rstd[:, fam, 4 * t:4 * t + 4].unsqueeze(2)
                                            .broadcast_to([P, HEADS, P]), ALU.mult).then_inc(o_scaled.sem, 1)
                        if s == OG_AT[i]:
                            dve.wait_ge(o_scaled.sem, o_scaled.at(b, i + 1))
                            dve.wait_ge(z_used.sem, z_used.at(b, i + 1))
                            V.tensor_tensor(o_tile, o_tile, v_g[:, t, :], ALU.mult).then_inc(og_ready.sem, 1)
                    for i in range(8):
                        if s == OT_AT[i]:
                            fam, t = divmod(i, 4)
                            dve.wait_ge(o_hi_done.sem, o_hi_done.at(b, i + 1))
                            frames = slice(t * P, (t + 1) * P)
                            V.scalar_tensor_tensor(
                                out=o_lo[:, 4 * fam:4 * fam + 4, frames],
                                in0=OT_BANK[i][:, :].rearrange("p (a n) -> p a n", a=4),
                                scalar=nw[:, fam:fam + 1],
                                in1=o_hi[:, 4 * fam:4 * fam + 4, frames].bitcast(fp32),
                                op0=ALU.mult, op1=ALU.subtract).then_inc(o_split.sem, 1)
                    if not last:
                        if s == XR_AT - 1:
                            root_diagonals(b + 1)
                        for j in range(4):
                            if s == XN_AT[j]:
                                x_scale(b + 1, j)
                            if s == XN_AT[j] + 1:
                                h_low(b + 1, j)
                    if s == 59:
                        for t in range(NT):
                            dve.wait_ge(y_rstd.sem, y_rstd.at(b, t + 1))
                            V.scalar_tensor_tensor(out=xy[:, t, :], in0=xy[:, t, :], scalar=y_rs[:, t:t + 1],
                                                   in1=fnw_bc[:, :], op0=ALU.mult,
                                                   op1=ALU.mult).then_inc(y_ready.sem, 1)
                assert last or link_at[1] == DVE_LINKS, f"DVE_LINKS {link_at[1]}"

            with dve.Fori(0, NB - 1) as b:
                body(b, False)
            body(NB - 1, True)

        @block.tensor
        def _(pe):
            mm, tr = nc.tensor.matmul, nc.tensor.transpose

            ADA_BANK = A + A[2:4]

            def root_rows(nb):
                pe.wait_ge(x_diag.sem, x_diag.at(nb, 1))
                mm(R[0][:, :], one[:, :].broadcast_to([P, P]), h_tmp[:, 0:NT, :].rearrange("p t n -> p (t n)"),
                   start=True, stop=True).then_inc(xr_done.sem, 1)

            def modulation(n):
                pe.wait_ge(ada_in[n % 4][1], 16 * (n // 4 + 1))
                if n >= 4:
                    pe.wait_ge(mod_copied, n - 1)
                if ADA_DVE[n] < 4:
                    pe.wait_ge(ada_in[n % 4][0], 16 * (n // 4 + 1))
                for k in range(ADA_DVE[n], KT):
                    mm(ADA_BANK[n][:, :], c_act[:, k:k + 1].broadcast_to([P, P]), ada_w[n % 4][:, k, :],
                       start=(k == ADA_DVE[n]), stop=False)
                pe.wait_ge(ada_sum, n + 1)
                mm(ADA_BANK[n][:, :], one[:, :].broadcast_to([P, P]), ada_w[n % 4][:, 0, :],
                   start=False, stop=True).then_inc(ada_pe, 1)

            def mod_transpose(n):
                pe.wait_ge(mod_copied, n + 1)
                if n >= 2:
                    pe.wait_ge(mod_col, n - 1)
                for k in range(4):
                    last = tr(F[n % 2][:, k * P:(k + 1) * P], mod_row[:, (4 * n + k) * P:(4 * n + k + 1) * P],
                              ident[:, :])
                last.then_inc(modT, 1)

            pe.wait_ge(c_ready, 1)
            modulation(0)
            modulation(1)
            pe.wait_ge(consts, 1)
            mod_transpose(0)
            modulation(2)
            mod_transpose(1)
            mod_transpose(2)
            modulation(3)
            mod_transpose(3)
            root_rows(0)
            modulation(4)
            modulation(5)

            PASSES = ((0, 0), (0, 1), (1, 0))
            h_, w_, o_, m_ = (h_hi, h_lo), (w_hi, w_lo), (o_hi, o_lo), (m_hi, m_lo)

            def token_major(b, s, part, parts, k_per, width, src, free, free_n=(1, 2, 3, 4)):
                if s < GK0:
                    pe.wait_ge(h_split.sem, h_split.at(b, s + 1))
                for t in range(NT):
                    if part == 0:
                        pe.wait_ge(free.sem, free.at(b, free_n[t]))
                    for kk in range(k_per):
                        k = part * k_per + kk
                        for n, (ia, iw) in enumerate(PASSES):
                            last = mm(A[t][:, 0:width], src[ia][:, k, t * P:(t + 1) * P],
                                      w_[iw][:, s % RING, kk * width:(kk + 1) * width],
                                      start=(k == 0 and n == 0), stop=(k == KT - 1 and n == 2))
                    if t == NT - 1:
                        last.then_inc(slot_done.sem, 1)
                    elif part == parts - 1:
                        last.then_inc(a_done.sem, 1)

            def feature_major(b, s, dst):
                for k in range(KT):
                    for n, (iw, ia) in enumerate(PASSES):
                        last = mm(dst[:, :], w_[iw][:, s % RING, k * P:(k + 1) * P], h_[ia][:, k, :],
                                  start=(k == 0 and n == 0), stop=(k == KT - 1 and n == 2))
                last.then_inc(slot_done.sem, 1)

            def slot(b, s):
                if s == 19:
                    pe.wait_ge(a_rows_ready.sem, a_rows_ready.at(b, 2))
                pe.wait_ge(w_split.sem, w_split.at(b, s + 1))
                if s < GK0:
                    token_major(b, s, s - F0, 4, 2, 512, h_, out_used, (-3, -2, -1, 0))
                elif s < I0:
                    token_major(b, s, s - GK0, 2, 4, GW, h_, f_copied)
                elif s < GV0:
                    token_major(b, s, s - I0, 4, 2, 512, h_, gk_copied)
                elif s < GQ0:
                    token_major(b, s, s - GV0, 4, 2, 512, h_, i_copied)
                elif s < HQ0:
                    n = s - GQ0
                    pe.wait_ge(mg_used.sem, mg_used.at(b, n - 1))
                    feature_major(b, s, F[n])
                elif s < GZ0:
                    n = s - HQ0
                    if n < 2:
                        pe.wait_ge(gq_used.sem, gq_used.at(b, n + 1))
                    else:
                        pe.wait_ge(hq_used.sem, hq_used.at(b, n - 1))
                    feature_major(b, s, F[n % 2])
                elif s < HZ0:
                    token_major(b, s, s - GZ0, 4, 2, 512, h_, gv_copied)
                elif s < MG0:
                    token_major(b, s, s - HZ0, 4, 2, 512, h_, z_used)
                elif s in MG_SLOT:
                    j, g = MG_SLOT[s]
                    if j == 0:
                        pe.wait_ge(o_copied.sem, o_copied.at(b, (5, 7)[g]))
                    else:
                        pe.wait_ge(mg_used.sem, mg_used.at(b, 2 * j + g - 1))
                    feature_major(b, s, F[g])
                elif s in UP_SLOT:
                    j = UP_SLOT[s]
                    if j == 0:
                        pe.wait_ge(o_split.sem, o_split.at(b, 8))
                    elif j >= 2:
                        pe.wait_ge(up_used.sem, up_used.at(b, j - 1))
                    for g in range(2):
                        for k in range(HEADS):
                            for n, (iw, ia) in enumerate(PASSES):
                                kk = 4 * g + k
                                last = mm(A[2 * (j % 2) + g][:, :], w_[iw][:, s % RING, kk * P:(kk + 1) * P],
                                          o_[ia][:, kk, :], start=(k == 0 and n == 0),
                                          stop=(k == HEADS - 1 and n == 2))
                    last.then_inc(slot_done.sem, 1)
                else:
                    n, part = divmod(s - OUT0, 4)
                    if n == 0:
                        pe.wait_ge(m_split.sem, m_split.at(b, 2 * part + 2))
                        token_major(b, s, part, 4, 2, 512, m_, up_used, (7, 7, 8, 8))
                    else:
                        token_major(b, s, part, 4, 2, 512, m_, out_used)

            def increments(b, i):
                fam, t = divmod(i, 4)
                if i == 0:
                    pe.wait_ge(a_ready.sem, a_ready.at(b, 1))
                    pe.wait_ge(kdec_g_ready.sem, kdec_g_ready.at(b, 1))
                if i == 4:
                    pe.wait_ge(kdec_h_ready.sem, kdec_h_ready.at(b, 1))
                for g in range(2 if fam == 0 else 4):
                    n = GKW if fam == 0 else P
                    for c in range(2):
                        fr = slice(c * CHUNK, (c + 1) * CHUNK)
                        k_, v_ = (gklr, v_g) if fam == 0 else (kdec_h, v_h)
                        last = mm(R[c][:, g * n:(g + 1) * n], k_[fr, t, g * P:(g + 1) * P],
                                  v_[fr, t, g * n:(g + 1) * n], start=True, stop=True)
                last.then_inc(dS_done.sem, 1)

            def outputs(b, i):
                fam, t = divmod(i, 4)
                pe.wait_ge(S_ready.sem, S_ready.at(b, i + 1))
                if i == 0:
                    pe.wait_ge(hq_used.sem, hq_used.at(b, 4))
                elif i < 7:
                    pe.wait_ge(o_copied.sem, o_copied.at(b, i if i == 6 else max(i - 1, 1)))
                dst = O_BANK[i]
                for g in range(2 if fam == 0 else 4):
                    n = GKW if fam == 0 else P
                    for c in range(2):
                        fr = slice(t * P + c * CHUNK, t * P + (c + 1) * CHUNK)
                        q_, S_ = ((q_g, S_g[:, c, g, :, :].rearrange("p r n -> p (r n)")) if fam == 0
                                  else (q_h, S_h[:, c, g, :]))
                        last = mm(dst[c * CHUNK:(c + 1) * CHUNK, g * n:(g + 1) * n], q_[:, g, fr], S_,
                                  start=True, stop=True)
                last.then_inc(o_done.sem, 1)

            def o_transpose(b, i):
                fam, t = divmod(i, 4)
                pe.wait_ge(og_ready.sem, og_ready.at(b, i + 1))
                if i == 0:
                    pe.wait_ge(z_used.sem, z_used.at(b, 8))
                if i == 4:
                    pe.wait_ge(o_copied.sem, o_copied.at(b, 8))
                if i >= 6:
                    pe.wait_ge(o_split.sem, o_split.at(b, i - 5))
                for g in range(4):
                    last = tr(OT_BANK[i][:, g * P:(g + 1) * P],
                              o_tm[:, t, fam * 512 + g * P:fam * 512 + (g + 1) * P], ident[:, :])
                last.then_inc(oT_done.sem, 1)

            def hosted(b, s, last_block):
                if s == 6:
                    pe.wait_ge(gk_copied.sem, gk_copied.at(b, 4))
                    for t in range(NT):
                        last = tr(R[0][0:LR, t * P:(t + 1) * P], gklr[:, t, GKW:GW], ident[:, :])
                    last.then_inc(lrT_done.sem, 1)
                if s == 8:
                    pe.wait_ge(lrT_copied.sem, lrT_copied.at(b, 1))
                    for t in range(NT):
                        last = mm(R[t // 2][:, (t % 2) * GKW:(t % 2 + 1) * GKW], lrT[:, t * P:(t + 1) * P],
                                  wa2[:, :], start=True, stop=True)
                    last.then_inc(y_done.sem, 1)
                if s in (14, 15):
                    if s == 14:
                        pe.wait_ge(lf_split.sem, lf_split.at(b, 1))
                        pe.wait_ge(y_added.sem, y_added.at(b, 1))
                    for t in (0, 1) if s == 14 else (2, 3):
                        if t >= 2:
                            pe.wait_ge(grev_h_used.sem, grev_h_used.at(b, t - 1))
                        mm(R[t % 2][:, :], tri[:, 0, :], lf_hi[:, t, :], start=True, stop=False)
                        mm(R[t % 2][:, :], tri[:, 0, :], lf_lo[:, t, :], start=False,
                           stop=True).then_inc(grev_h_done.sem, 1)
                if s == 16:
                    pe.wait_ge(grev_h_used.sem, grev_h_used.at(b, 4))
                    pe.wait_ge(la_split.sem, la_split.at(b, 1))
                    for t in range(NT):
                        dst = R[t // 2][:, (t % 2) * GKW:(t % 2 + 1) * GKW]
                        mm(dst, tri[:, 1, :], la_hi[:, t, :], start=True, stop=False)
                        last = mm(dst, tri[:, 1, :], la_lo[:, t, :], start=False, stop=True)
                    last.then_inc(grev_g_done.sem, 1)
                if s == 17:
                    pe.wait_ge(kexp_g.sem, kexp_g.at(b, 2))
                    for bank_, v, n, halves in ((R[0], 0, 512, (lf_hi, lf_lo)), (R[1], 1, GKW, (la_hi, la_lo))):
                        for t in range(NT):
                            for q, half in enumerate(halves):
                                last = mm(bank_[0:NC_BLK, 0:n], ind[:, v, t, :], half[:, t, :],
                                          start=(t == 0 and q == 0), stop=(t == NT - 1 and q == 1))
                    last.then_inc(gend_done.sem, 1)
                if s == 19:
                    for i in range(6):
                        last = tr(R[0][:, i * NC_BLK:(i + 1) * NC_BLK], a_rows[:, i * P:(i + 1) * P],
                                  ident[0:NC_BLK, 0:NC_BLK])
                    last.then_inc(aT_done.sem, 1)
                for i in range(8):
                    if s == STEP_AT[i] + 1:
                        outputs(b, i)
                for i in range(8):
                    if s == STEP_AT[i]:
                        increments(b, i)
                for i in range(8):
                    if s == OT_AT[i]:
                        o_transpose(b, i)
                if not last_block and s == XR_AT:
                    root_rows(b + 1)

            def body(b, last):
                for s in range(SLOTS):
                    slot(b, s)
                    hosted(b, s, last)

            with pe.Fori(0, NB - 1) as b:
                body(b, False)
            body(NB - 1, True)


def layout(np, inp):
    x = np.ascontiguousarray(inp["x"])
    n = x.shape[1]
    w = inp["w_in"][0]
    at, part = 0, {}
    for name, width in (("gq", 256), ("gk", 256), ("gv", 512), ("gz", 512), ("lr", 16), ("hq", 512),
                        ("hf", 512), ("hi", 512), ("hz", 512), ("mg", 2048)):
        part[name] = w[:, at:at + width]
        at += width
    stream = np.zeros((SLOTS, P, SLOT_W), w.dtype)

    def put(s, m):
        k = m.shape[0] // P
        stream[s, :, 0:k * m.shape[1]] = m.reshape(k, P, -1).transpose(1, 0, 2).reshape(P, -1)

    for s0, m, parts in ((F0, part["hf"], 4), (GK0, np.concatenate([part["gk"], part["lr"]], 1), 2),
                         (I0, part["hi"], 4), (GV0, part["gv"], 4), (GZ0, part["gz"], 4),
                         (HZ0, part["hz"], 4), (OUT0, inp["w_out"][0][:, 0:512], 4),
                         (OUT0 + 4, inp["w_out"][0][:, 512:1024], 4)):
        for i in range(parts):
            put(s0 + i, m[i * (D // parts):(i + 1) * (D // parts)])
    for i in range(2):
        put(GQ0 + i, part["gq"][:, i * P:(i + 1) * P])
    for i in range(4):
        put(HQ0 + i, part["hq"][:, i * P:(i + 1) * P])
    for s, (j, g) in MG_SLOT.items():
        put(s, part["mg"][:, g * D + j * P:g * D + (j + 1) * P])
    up = np.concatenate([inp["w_up_gla"][0], inp["w_up_hgrn"][0]], 0)
    for s, j in UP_SLOT.items():
        put(s, up[:, j * P:(j + 1) * P])

    def as_cols(v):
        return v.reshape(-1, P).T

    cols = np.concatenate([as_cols(inp["c"][0]), as_cols(inp["norm_w"][0]), as_cols(inp["merge_b"][0]),
                           as_cols(inp["gla_norm_w"][0]), as_cols(inp["hgrn_norm_w"][0]),
                           as_cols(inp["ada_b"][0][0:2 * D])], 1)
    rows = np.concatenate([inp["hgrn_gamma"][0], inp["gla_ba"][0], inp["final_norm_w"], inp["ada_b"][0]])[None]
    ada = inp["ada_w"][0].reshape(KT, P, 6, 512).transpose(2, 1, 0, 3).reshape(6, P, KT * 512)
    xt = x.reshape(n // T, T, KT, P).transpose(0, 3, 2, 1).reshape(n // T * P, KT * T)
    return {"x": x.reshape(n, D), "xt": xt, "wa2": inp["gla_wa2"][0], "cols": cols, "rows": rows,
            "w_stream": stream, "ada": ada}


def kernel(**inputs):
    import numpy as np
    import concourse.bacc as bacc
    from concourse.bass_utils import run_bass_kernel_spmd

    inp = {k: np.asarray(v) for k, v in inputs.items()}
    nc = bacc.Bacc("TRN2", target_bir_lowering=False, num_devices=1)
    arrays, aps = {}, {}
    for name, a in layout(np, inp).items():
        a = np.ascontiguousarray(a)
        arrays[f"in_{name}"] = a
        aps[name] = nc.dram_tensor(f"in_{name}", a.shape, mybir.dt.from_np(a.dtype), kind="ExternalInput").ap()
    out = nc.dram_tensor("result", list(aps["x"].shape), mybir.dt.float32, kind="ExternalOutput").ap()
    build(nc, aps["x"], aps["xt"], aps["wa2"], aps["cols"], aps["rows"], aps["w_stream"], aps["ada"], out)
    r = run_bass_kernel_spmd(nc, [arrays], core_ids=[0])
    return r.results[0]["result"].reshape(inp["x"].shape)
```
